# Optimizing a Trainium2 kernel written in Bass

```python
import jax, jax.numpy as jnp
from jax import lax
import numpy as np
import math

D_MODEL = 1024
BATCH = 1
SEQ = 512
DEPTH = 2

HEAD_DIM = 64
RET_HEADS = 8
DIL_HEADS = 8
SB_HEADS = D_MODEL // HEAD_DIM
RET_WIDTH = RET_HEADS * HEAD_DIM
DIL_WIDTH = DIL_HEADS * HEAD_DIM
SB_WIDTH = SB_HEADS * HEAD_DIM
HYB_IN = 4 * RET_WIDTH + 3 * DIL_WIDTH
D_FF = 2816
BLOCK = 128
RET_CHUNK = 128
RET_ROPE_THETA = 10000.0
ROPE_THETA = 500000.0
ROPE_DIM = HEAD_DIM // 4
DILATED_PATTERNS = ((128, 1), (512, 4), (2048, 16))
NORM_EPS = 1e-6
GN_EPS = 1e-5
N_EVEN = (DEPTH + 1) // 2
N_ODD = DEPTH // 2


def rms_norm(x, g):
    xf = x.astype(jnp.float32)
    y = xf * lax.rsqrt(jnp.mean(xf * xf, axis=-1, keepdims=True) + NORM_EPS)
    return (y * g.astype(jnp.float32)).astype(x.dtype)

def swiglu_ffn(x, g, w_in, w_out):
    h = rms_norm(x, g)
    gate, up = jnp.split(h @ w_in, 2, axis=-1)
    return (jax.nn.silu(gate) * up) @ w_out

def split_heads(t, n_heads):
    b, s, _ = t.shape
    return t.reshape(b, s, n_heads, HEAD_DIM).transpose(0, 2, 1, 3)

def merge_heads(t):
    b, h, s, dh = t.shape
    return t.transpose(0, 2, 1, 3).reshape(b, s, h * dh)

def rotary(x, rot_dim, theta):
    s = x.shape[-2]
    half = rot_dim // 2
    inv_freq = 1.0 / (theta ** (jnp.arange(half, dtype=jnp.float32) / half))
    ang = jnp.arange(s, dtype=jnp.float32)[:, None] * inv_freq[None, :]
    cos, sin = jnp.cos(ang), jnp.sin(ang)
    xr = x[..., :rot_dim].astype(jnp.float32)
    x1, x2 = xr[..., :half], xr[..., half:]
    rot = jnp.concatenate([x1 * cos - x2 * sin, x2 * cos + x1 * sin], axis=-1).astype(x.dtype)
    return jnp.concatenate([rot, x[..., rot_dim:]], axis=-1)

def retention_chunkwise(q, k, v):
    b, h, s, dk = q.shape
    c = RET_CHUNK
    nc = s // c
    out_dtype = v.dtype
    q, k, v = (t.astype(jnp.float32) for t in (q, k, v))
    k = k * (dk ** -0.5)
    log_g = jnp.log(1.0 - 2.0 ** (-5.0 - jnp.arange(h, dtype=jnp.float32)))
    i = jnp.arange(c, dtype=jnp.float32)
    diff = i[:, None] - i[None, :]
    decay_in = jnp.where(diff >= 0, jnp.exp(jnp.maximum(diff, 0.0)[None] * log_g[:, None, None]), 0.0)
    qc = q.reshape(b, h, nc, c, dk)
    kc = k.reshape(b, h, nc, c, dk)
    vc = v.reshape(b, h, nc, c, -1)
    scores = jnp.einsum('bhnid,bhnjd->bhnij', qc, kc) * decay_in[None, :, None]
    inner = jnp.einsum('bhnij,bhnje->bhnie', scores, vc)
    k_decay = jnp.exp((c - 1 - i)[None, :] * log_g[:, None])
    kv = jnp.einsum('bhnjd,bhnje->nbhde', kc * k_decay[None, :, None, :, None], vc)
    chunk_decay = jnp.exp(c * log_g)[None, :, None, None]

    def step(state, kv_n):
        return state * chunk_decay + kv_n, state

    _, state_prev = lax.scan(step, jnp.zeros_like(kv[0]), kv)
    q_decay = jnp.exp((i + 1)[None, :] * log_g[:, None])
    cross = jnp.einsum('bhnid,nbhde->bhnie', qc * q_decay[None, :, None, :, None], state_prev)
    return (inner + cross).reshape(b, h, s, -1).astype(out_dtype)

def head_group_norm(o, g):
    of = o.astype(jnp.float32)
    mu = jnp.mean(of, axis=-1, keepdims=True)
    var = jnp.mean(jnp.square(of - mu), axis=-1, keepdims=True)
    y = (of - mu) * lax.rsqrt(var + GN_EPS)
    y = y * g.astype(jnp.float32).reshape(o.shape[1], 1, o.shape[3])
    return y.astype(o.dtype)

def band_attention(q, k, v, n_back):
    *lead, l_len, dh = q.shape
    nb = l_len // BLOCK
    qb = q.reshape(*lead, nb, BLOCK, dh)

    def with_prev(t):
        tb = t.reshape(*lead, nb, BLOCK, dh)
        prev = jnp.concatenate([jnp.zeros_like(tb[..., :1, :, :]), tb[..., :-1, :, :]], axis=-3)
        return jnp.concatenate([prev, tb], axis=-2)

    kb, vb = with_prev(k), with_prev(v)
    s = jnp.einsum('...nqd,...nkd->...nqk', qb, kb).astype(jnp.float32) * (dh ** -0.5)
    dist = (jnp.arange(BLOCK)[:, None] + BLOCK) - jnp.arange(2 * BLOCK)[None, :]
    in_band = (dist >= 0) & (dist <= n_back)
    key_pos = jnp.arange(nb)[:, None] * BLOCK - BLOCK + jnp.arange(2 * BLOCK)[None, :]
    mask = in_band[None] & (key_pos >= 0)[:, None, :]
    s = jnp.where(mask, s, -jnp.inf)
    m = jnp.max(s, axis=-1, keepdims=True)
    p = jnp.exp(s - m)
    den = jnp.sum(p, axis=-1, keepdims=True)
    o = jnp.einsum('...nqk,...nkd->...nqd', p, vb.astype(jnp.float32)) / den
    lse = (m + jnp.log(den))[..., 0]
    return o.reshape(*lead, l_len, dh), lse.reshape(*lead, l_len)

def dilated_attention(q, k, v):
    b, h, s, dh = q.shape
    outs, lses = [], []
    for window, dil in DILATED_PATTERNS:
        mult = dil * BLOCK
        s_pad = -(-s // mult) * mult
        pad = ((0, 0), (0, 0), (0, s_pad - s), (0, 0))

        def by_residue(t):
            return jnp.pad(t, pad).reshape(b, h, s_pad // dil, dil, dh).transpose(0, 1, 3, 2, 4)

        o, lse = band_attention(by_residue(q), by_residue(k), by_residue(v), window // dil)
        outs.append(o.transpose(0, 1, 3, 2, 4).reshape(b, h, s_pad, dh)[:, :, :s])
        lses.append(lse.transpose(0, 1, 3, 2).reshape(b, h, s_pad)[:, :, :s])
    w = jax.nn.softmax(jnp.stack(lses, axis=0), axis=0)
    o = jnp.sum(w[..., None] * jnp.stack(outs, axis=0), axis=0)
    return o.astype(q.dtype)

def stick_breaking_attention(q, k, v):
    b, h, s, dh = q.shape
    nb = s // BLOCK
    kf, vf = k.astype(jnp.float32), v.astype(jnp.float32)
    key_pos = jnp.arange(s)

    def one_block(args):
        q_blk, blk = args
        z = jnp.einsum('bhqd,bhkd->bhqk', q_blk.astype(jnp.float32), kf) * (dh ** -0.5)
        q_pos = blk * BLOCK + jnp.arange(BLOCK)
        causal = key_pos[None, :] < q_pos[:, None]
        log_stay = jnp.where(causal, jax.nn.log_sigmoid(-z), 0.0)
        later = lax.cumsum(log_stay, axis=3, reverse=True) - log_stay
        a = jnp.where(causal, jnp.exp(jax.nn.log_sigmoid(z) + later), 0.0)
        return jnp.einsum('bhqk,bhkd->bhqd', a, vf)

    q_blocks = q.reshape(b, h, nb, BLOCK, dh).transpose(2, 0, 1, 3, 4)
    o = lax.map(one_block, (q_blocks, jnp.arange(nb)))
    return o.transpose(1, 2, 0, 3, 4).reshape(b, h, s, dh).astype(q.dtype)

def retention_dilated_mixer(x, norm_g, w_in, ret_gn, w_out):
    h = rms_norm(x, norm_g)
    proj = h @ w_in
    cuts = [RET_WIDTH, 2 * RET_WIDTH, 3 * RET_WIDTH, 4 * RET_WIDTH,
            4 * RET_WIDTH + DIL_WIDTH, 4 * RET_WIDTH + 2 * DIL_WIDTH]
    rq, rk, rv, rg, dq, dk, dv = jnp.split(proj, cuts, axis=-1)
    rq = rotary(split_heads(rq, RET_HEADS), HEAD_DIM, RET_ROPE_THETA)
    rk = rotary(split_heads(rk, RET_HEADS), HEAD_DIM, RET_ROPE_THETA)
    ret = retention_chunkwise(rq, rk, split_heads(rv, RET_HEADS))
    ret = merge_heads(head_group_norm(ret, ret_gn)) * jax.nn.silu(rg)
    dq = rotary(split_heads(dq, DIL_HEADS), ROPE_DIM, ROPE_THETA)
    dk = rotary(split_heads(dk, DIL_HEADS), ROPE_DIM, ROPE_THETA)
    dil = merge_heads(dilated_attention(dq, dk, split_heads(dv, DIL_HEADS)))
    return jnp.concatenate([ret, dil], axis=-1) @ w_out

def stick_breaking_mixer(x, norm_g, w_in, w_out):
    h = rms_norm(x, norm_g)
    q, k, v = jnp.split(h @ w_in, 3, axis=-1)
    o = stick_breaking_attention(split_heads(q, SB_HEADS), split_heads(k, SB_HEADS), split_heads(v, SB_HEADS))
    return merge_heads(o) @ w_out

def first_inputs(seed: int = 0) -> dict:
    key = jax.random.key(seed)
    ks = jax.random.split(key, 16)
    f32 = jnp.float32

    def gain(k, shape):
        return 1.0 + 0.02 * jax.random.normal(k, shape, f32)

    def dense(k, shape, fan_in):
        return jax.random.normal(k, shape, f32) * (fan_in ** -0.5)

    return {
        'x': jax.random.normal(ks[0], (BATCH, SEQ, D_MODEL), f32),
        'ffn1_norm': gain(ks[1], (DEPTH, D_MODEL)),
        'ffn1_w_in': dense(ks[2], (DEPTH, D_MODEL, 2 * D_FF), D_MODEL),
        'ffn1_w_out': dense(ks[3], (DEPTH, D_FF, D_MODEL), D_FF),
        'mix_norm': gain(ks[4], (DEPTH, D_MODEL)),
        'ffn2_norm': gain(ks[5], (DEPTH, D_MODEL)),
        'ffn2_w_in': dense(ks[6], (DEPTH, D_MODEL, 2 * D_FF), D_MODEL),
        'ffn2_w_out': dense(ks[7], (DEPTH, D_FF, D_MODEL), D_FF),
        'hyb_w_in': dense(ks[8], (N_EVEN, D_MODEL, HYB_IN), D_MODEL),
        'ret_gn': gain(ks[9], (N_EVEN, RET_WIDTH)),
        'hyb_w_out': dense(ks[10], (N_EVEN, RET_WIDTH + DIL_WIDTH, D_MODEL), RET_WIDTH + DIL_WIDTH),
        'sb_w_in': dense(ks[11], (N_ODD, D_MODEL, 3 * SB_WIDTH), D_MODEL),
        'sb_w_out': dense(ks[12], (N_ODD, SB_WIDTH, D_MODEL), SB_WIDTH),
        'final_norm': gain(ks[13], (D_MODEL,)),
    }

def first_block(x, ffn1_norm, ffn1_w_in, ffn1_w_out, mix_norm, ffn2_norm, ffn2_w_in, ffn2_w_out,
              hyb_w_in, ret_gn, hyb_w_out, sb_w_in, sb_w_out, final_norm):
    for layer in range(DEPTH):
        x = x + 0.5 * swiglu_ffn(x, ffn1_norm[layer], ffn1_w_in[layer], ffn1_w_out[layer])
        if layer % 2 == 0:
            e = layer // 2
            x = x + retention_dilated_mixer(x, mix_norm[layer], hyb_w_in[e], ret_gn[e], hyb_w_out[e])
        else:
            o = layer // 2
            x = x + stick_breaking_mixer(x, mix_norm[layer], sb_w_in[o], sb_w_out[o])
        x = x + 0.5 * swiglu_ffn(x, ffn2_norm[layer], ffn2_w_in[layer], ffn2_w_out[layer])
    return rms_norm(x, final_norm)


MIX_WIDTH = D_MODEL
POOL_WIDTH = D_MODEL // 2
POOL_WINDOWS = (2, 4, 8, 16)
POOL_GROUPS = len(POOL_WINDOWS)
POOL_GC = POOL_WIDTH // POOL_GROUPS
NSA_HEADS = (MIX_WIDTH - POOL_WIDTH) // HEAD_DIM
KV_GROUPS = 2
HEADS_PER_GROUP = NSA_HEADS // KV_GROUPS
N_BRANCH = 3
CMP_LEN = 32
CMP_STRIDE = 16
SEL_LEN = 64
SEL_TOPN = 16
WINDOW = 512
Q_BLOCK = 128
D_FF_2 = 4 * D_MODEL
ROPE_THETA_2 = 10000.0
EPS = 1e-6
NEG = -1e30
FORCED_SCORE = 1e4

Q_COLS = NSA_HEADS * HEAD_DIM
KV_COLS = KV_GROUPS * HEAD_DIM
GATE_COLS = NSA_HEADS * N_BRANCH
IN_COLS = POOL_WIDTH + Q_COLS + 2 * N_BRANCH * KV_COLS + GATE_COLS


def rms_norm_2(x, g):
    xf = x.astype(jnp.float32)
    y = xf * lax.rsqrt(jnp.mean(xf * xf, axis=-1, keepdims=True) + EPS)
    return (y * g.astype(jnp.float32)).astype(x.dtype)

def rope(x, pos):
    dk = x.shape[-1]
    half = dk // 2
    inv = ROPE_THETA_2 ** (-jnp.arange(half, dtype=jnp.float32) * 2.0 / dk)
    ang = pos.astype(jnp.float32)[:, None] * inv[None, :]
    shape = (1, pos.shape[0]) + (1,) * (x.ndim - 3) + (half,)
    cos = jnp.cos(ang).reshape(shape)
    sin = jnp.sin(ang).reshape(shape)
    xf = x.astype(jnp.float32)
    x1, x2 = xf[..., :half], xf[..., half:]
    return jnp.concatenate([x1 * cos - x2 * sin, x2 * cos + x1 * sin], axis=-1).astype(x.dtype)

def pool_mixer(u, pool_w, pool_scale):
    B, S, _ = u.shape
    ug = u.reshape(B, S, POOL_GROUPS, POOL_GC).astype(jnp.float32)
    cs = jnp.concatenate([jnp.zeros((B, 1, POOL_GROUPS, POOL_GC), jnp.float32),
                          jnp.cumsum(ug, axis=1)], axis=1)
    t = jnp.arange(S)
    win = jnp.array(POOL_WINDOWS, dtype=jnp.int32)
    lower = jnp.maximum(t[:, None] + 1 - win[None, :], 0)
    count = jnp.minimum(t[:, None] + 1, win[None, :]).astype(jnp.float32)
    gidx = jnp.arange(POOL_GROUPS)[None, :]
    sums = cs[:, 1:] - cs[:, lower, gidx]
    pooled = (sums / count[None, :, :, None] - ug).astype(u.dtype)
    y = jnp.einsum('bsgc,gcd->bsgd', pooled, pool_w)
    return y.reshape(B, S, POOL_WIDTH) * pool_scale

def compress(t, pe, w1, w2, blk):
    B = t.shape[0]
    n_cmp = blk.shape[0]
    tb = t[:, blk] + pe[None, None, :, None, :]
    flat = tb.transpose(0, 1, 3, 2, 4).reshape(B, n_cmp, KV_GROUPS, CMP_LEN * HEAD_DIM)
    return jax.nn.silu(flat @ w1) @ w2

def nsa_mixer(q, k_all, v_all, gates, q_norm, k_norm, cmp_pe, cmp_w1, cmp_w2):
    B, S = q.shape[0], q.shape[1]
    G, Hg, dk = KV_GROUPS, HEADS_PER_GROUP, HEAD_DIM
    scale = 1.0 / math.sqrt(dk)
    pos = jnp.arange(S)

    q = rope(rms_norm_2(q, q_norm), pos).reshape(B, S, G, Hg, dk)
    k_s = rope(rms_norm_2(k_all[:, :, 1], k_norm[1]), pos)
    k_w = rope(rms_norm_2(k_all[:, :, 2], k_norm[2]), pos)
    v_s = v_all[:, :, 1]
    v_w = v_all[:, :, 2]

    n_cmp = (S - CMP_LEN) // CMP_STRIDE + 1
    blk = np.arange(n_cmp)[:, None] * CMP_STRIDE + np.arange(CMP_LEN)[None, :]
    cmp_end = jnp.arange(n_cmp) * CMP_STRIDE + (CMP_LEN - 1)
    k_cmp = compress(k_all[:, :, 0], cmp_pe[0], cmp_w1[0], cmp_w2[0], blk)
    v_cmp = compress(v_all[:, :, 0], cmp_pe[1], cmp_w1[1], cmp_w2[1], blk)
    k_cmp = rope(rms_norm_2(k_cmp, k_norm[0]), cmp_end)
    s_c = jnp.einsum('bsghd,bngd->bsghn', q, k_cmp).astype(jnp.float32) * scale
    mask_c = (cmp_end[None, :] <= pos[:, None])[None, :, None, None, :]
    p_c = jax.nn.softmax(jnp.where(mask_c, s_c, NEG), axis=-1)
    p_c = jnp.where(mask_c, p_c, 0.0)
    o_cmp = jnp.einsum('bsghn,bngd->bsghd', p_c.astype(v_cmp.dtype), v_cmp)

    n_sel = S // SEL_LEN
    cs0 = np.arange(n_cmp) * CMP_STRIDE
    ss0 = np.arange(n_sel) * SEL_LEN
    ov = np.minimum(cs0[:, None] + CMP_LEN, ss0[None, :] + SEL_LEN) - np.maximum(cs0[:, None], ss0[None, :])
    ov_mat = jnp.asarray(np.clip(ov, 0, None).astype(np.float32) / CMP_LEN)
    imp = jnp.einsum('bsghn,nj->bsgj', p_c, ov_mat)
    blk_id = jnp.arange(n_sel)[None, :]
    cur = (pos // SEL_LEN)[:, None]
    causal = blk_id <= cur
    forced = (blk_id == 0) | (blk_id == cur) | (blk_id == cur - 1)
    imp = jnp.where(causal[None, :, None, :],
                    jnp.where(forced[None, :, None, :], FORCED_SCORE, imp), -1.0)
    topn = min(SEL_TOPN, n_sel)
    vals, sel_idx = lax.top_k(imp, topn)
    sel_valid = vals >= 0.0

    k_sb = k_s.reshape(B, n_sel, SEL_LEN, G, dk).transpose(0, 3, 1, 2, 4)
    v_sb = v_s.reshape(B, n_sel, SEL_LEN, G, dk).transpose(0, 3, 1, 2, 4)
    pad = ((0, 0), (WINDOW, 0), (0, 0), (0, 0))
    k_wp = jnp.pad(k_w, pad)
    v_wp = jnp.pad(v_w, pad)
    bi = jnp.arange(B)[:, None, None, None]
    gi = jnp.arange(G)[None, None, :, None]
    C = Q_BLOCK

    def block_fn(qb):
        start = qb * C
        qc = lax.dynamic_slice_in_dim(q, start, C, axis=1)
        tc = start + jnp.arange(C)
        idx = lax.dynamic_slice_in_dim(sel_idx, start, C, axis=1)
        val = lax.dynamic_slice_in_dim(sel_valid, start, C, axis=1)
        kg = k_sb[bi, gi, idx]
        vg = v_sb[bi, gi, idx]
        s = jnp.einsum('bcghd,bcgnld->bcghnl', qc, kg).astype(jnp.float32) * scale
        kpos = idx[..., None] * SEL_LEN + jnp.arange(SEL_LEN)
        m = (kpos <= tc[None, :, None, None, None]) & val[..., None]
        s = jnp.where(m[:, :, :, None], s, NEG)
        sh = s.shape
        p = jax.nn.softmax(s.reshape(sh[:4] + (sh[4] * sh[5],)), axis=-1).reshape(sh)
        o_s = jnp.einsum('bcghnl,bcgnld->bcghd', p.astype(vg.dtype), vg)
        kw = lax.dynamic_slice_in_dim(k_wp, start, C + WINDOW, axis=1)
        vw = lax.dynamic_slice_in_dim(v_wp, start, C + WINDOW, axis=1)
        kpos_w = start - WINDOW + jnp.arange(C + WINDOW)
        diff = tc[:, None] - kpos_w[None, :]
        mw = ((diff >= 0) & (diff < WINDOW) & (kpos_w[None, :] >= 0))[None, :, None, None, :]
        sw = jnp.einsum('bcghd,bkgd->bcghk', qc, kw).astype(jnp.float32) * scale
        pw = jax.nn.softmax(jnp.where(mw, sw, NEG), axis=-1)
        o_w = jnp.einsum('bcghk,bkgd->bcghd', pw.astype(vw.dtype), vw)
        return o_s, o_w

    o_s, o_w = lax.map(block_fn, jnp.arange(S // C))
    o_s = o_s.transpose(1, 0, 2, 3, 4, 5).reshape(B, S, G, Hg, dk)
    o_w = o_w.transpose(1, 0, 2, 3, 4, 5).reshape(B, S, G, Hg, dk)

    g = jax.nn.sigmoid(gates.astype(jnp.float32)).reshape(B, S, G, Hg, N_BRANCH).astype(q.dtype)
    o = g[..., 0:1] * o_cmp + g[..., 1:2] * o_s + g[..., 2:3] * o_w
    return o.reshape(B, S, NSA_HEADS * dk)

def hybrid_layer(x, mod, norm1, norm2, w_in, pool_w, pool_scale, q_norm, k_norm,
                 cmp_pe, cmp_w1, cmp_w2, w_out, w_ff1, w_ff2):
    B, S, _ = x.shape
    shift1, scale1, gate1, shift2, scale2, gate2 = jnp.split(mod[:, None, :], 6, axis=-1)
    h = rms_norm_2(x, norm1) * (1.0 + scale1) + shift1
    proj = h @ w_in
    o0 = POOL_WIDTH
    o1 = o0 + Q_COLS
    o2 = o1 + 2 * N_BRANCH * KV_COLS
    u = proj[..., :o0]
    q = proj[..., o0:o1].reshape(B, S, NSA_HEADS, HEAD_DIM)
    kv = proj[..., o1:o2].reshape(B, S, 2, N_BRANCH, KV_GROUPS, HEAD_DIM)
    gates = proj[..., o2:]
    y_pool = pool_mixer(u, pool_w, pool_scale)
    y_nsa = nsa_mixer(q, kv[:, :, 0], kv[:, :, 1], gates, q_norm, k_norm, cmp_pe, cmp_w1, cmp_w2)
    mix = jnp.concatenate([y_pool, y_nsa], axis=-1) @ w_out
    x = x + gate1 * mix
    h2 = rms_norm_2(x, norm2) * (1.0 + scale2) + shift2
    ff = jnp.square(jax.nn.relu(h2 @ w_ff1)) @ w_ff2
    return x + gate2 * ff

def second_inputs(seed: int = 0) -> dict:
    key = jax.random.key(seed)
    ks = jax.random.split(key, 20)
    f32 = jnp.float32
    L, D = DEPTH, D_MODEL
    nrm = lambda k, shape, s: jax.random.normal(k, shape, f32) * s
    return {
        "x": nrm(ks[0], (BATCH, SEQ, D), 1.0),
        "c": nrm(ks[1], (BATCH, D), 1.0),
        "w_mod": nrm(ks[2], (L, D, 6 * D), 0.5 * D ** -0.5),
        "b_mod": nrm(ks[3], (L, 6 * D), 0.01),
        "norm1": 1.0 + nrm(ks[4], (L, D), 0.05),
        "norm2": 1.0 + nrm(ks[5], (L, D), 0.05),
        "w_in": nrm(ks[6], (L, D, IN_COLS), D ** -0.5),
        "pool_w": nrm(ks[7], (L, POOL_GROUPS, POOL_GC, POOL_GC), POOL_GC ** -0.5),
        "pool_scale": 0.5 + nrm(ks[8], (L, POOL_WIDTH), 0.1),
        "q_norm": 1.0 + nrm(ks[9], (L, HEAD_DIM), 0.05),
        "k_norm": 1.0 + nrm(ks[10], (L, N_BRANCH, HEAD_DIM), 0.05),
        "cmp_pe": nrm(ks[11], (L, 2, CMP_LEN, HEAD_DIM), 0.5),
        "cmp_w1": nrm(ks[12], (L, 2, CMP_LEN * HEAD_DIM, HEAD_DIM), (CMP_LEN * HEAD_DIM) ** -0.5),
        "cmp_w2": nrm(ks[13], (L, 2, HEAD_DIM, HEAD_DIM), HEAD_DIM ** -0.5),
        "w_out": nrm(ks[14], (L, MIX_WIDTH, D), MIX_WIDTH ** -0.5),
        "w_ff1": nrm(ks[15], (L, D, D_FF_2), D ** -0.5),
        "w_ff2": nrm(ks[16], (L, D_FF_2, D), D_FF_2 ** -0.5),
    }

def second_block(x, c, w_mod, b_mod, norm1, norm2, w_in, pool_w, pool_scale, q_norm, k_norm,
              cmp_pe, cmp_w1, cmp_w2, w_out, w_ff1, w_ff2):
    c_act = jax.nn.silu(c)
    for l in range(DEPTH):
        mod = c_act @ w_mod[l] + b_mod[l]
        x = hybrid_layer(x, mod, norm1[l], norm2[l], w_in[l], pool_w[l], pool_scale[l],
                         q_norm[l], k_norm[l], cmp_pe[l], cmp_w1[l], cmp_w2[l],
                         w_out[l], w_ff1[l], w_ff2[l])
    return x


def setup_inputs(seed=0):
    out = dict(first_inputs(seed))
    for name, value in second_inputs(seed + 1).items():
        if name != "x":
            out[name + "_2"] = value
    return out


def reference(
    x, ffn1_norm, ffn1_w_in, ffn1_w_out, mix_norm, ffn2_norm, ffn2_w_in, ffn2_w_out, hyb_w_in,
    ret_gn, hyb_w_out, sb_w_in, sb_w_out, final_norm, c_2, w_mod_2, b_mod_2, norm1_2, norm2_2,
    w_in_2, pool_w_2, pool_scale_2, q_norm_2, k_norm_2, cmp_pe_2, cmp_w1_2, cmp_w2_2, w_out_2,
    w_ff1_2, w_ff2_2,
):
    x = first_block(
        x, ffn1_norm, ffn1_w_in, ffn1_w_out, mix_norm, ffn2_norm, ffn2_w_in, ffn2_w_out,
        hyb_w_in, ret_gn, hyb_w_out, sb_w_in, sb_w_out, final_norm,
    )
    return second_block(
        x, c_2, w_mod_2, b_mod_2, norm1_2, norm2_2, w_in_2, pool_w_2, pool_scale_2, q_norm_2,
        k_norm_2, cmp_pe_2, cmp_w1_2, cmp_w2_2, w_out_2, w_ff1_2, w_ff2_2,
    )


_drawn_inputs = setup_inputs


def setup_inputs(seed=0):
    import zlib

    import numpy as np

    out = dict(_drawn_inputs(seed))
    spreads = {}
    factors = {'ffn1_norm': 3.903,
     'ffn2_norm': 5.185,
     'ret_gn': 6.666,
     'final_norm': 2.67,
     'b_mod_2': 2.736,
     'norm1_2': 6.794,
     'q_norm_2': 8.0,
     'k_norm_2': 8.0}
    for name, (base, spread) in spreads.items():
        noise = np.random.default_rng([zlib.crc32(name.encode()), seed]).standard_normal(out[name].shape)
        drawn = base * np.exp(spread * noise) if base else spread * noise
        out[name] = __import__('jax').numpy.asarray(drawn.astype(out[name].dtype))
    for name, factor in factors.items():
        out[name] = (out[name] * factor).astype(out[name].dtype)
    return out
```

```python
import numpy as np
import concourse.bass as bass
from concourse import mybir
from contextlib import ExitStack


def two_block_kernel(nc, ins, out, stop=99):
    F32, F32R = mybir.dt.float32, mybir.dt.float32r
    ALU = mybir.AluOpType
    ACT = mybir.ActivationFunctionType
    AX = mybir.AxisListType
    T = 512
    KT = 8

    with ExitStack() as ctx:
        ops = []
        begin, end = [], []
        clock = {k: 0.0 for k in ("pe", "act", "dve", "pool", "sp")}
        always = {k: set() for k in clock}
        idle = {k: [(0.0, 1e9)] for k in ("act", "dve", "pool")}

        def flat(tokens, into):
            for tok in tokens:
                if isinstance(tok, (list, tuple)):
                    flat(tok, into)
                elif tok is not None:
                    into.add(tok)
            return into

        def ready(*tokens):
            return max((end[t] for t in flat(tokens, set())), default=0.0)

        def size(ap):
            return int(np.prod(ap.shape[1:]))

        def op(lane, call, *after, signal=True, cost=0.1, sem=None, tab=None):
            deps = flat(after, set(always[lane]))
            start = max((end[t] for t in deps), default=0.0) + 0.05
            if lane in idle:
                gaps = idle[lane]
                for n, (a, b) in enumerate(gaps):
                    if max(a, start) + cost <= b:
                        start = max(a, start)
                        gaps[n:n + 1] = [g for g in ((a, start), (start + cost, b)) if g[1] - g[0] > 0.08]
                        break
                del gaps[:-40]
                clock[lane] = gaps[-1][0]
            else:
                start = max(clock[lane], start)
                clock[lane] = start + (0.7 if sem else cost)
            ops.append((lane, call, deps, cost, sem, tab))
            begin.append(start)
            end.append(start + cost + 0.1)
            return len(ops) - 1

        def wait(lane, *tokens):
            flat(tokens, always[lane])

        def all_done():
            ops.append((None, None, set(range(joined[0], len(ops))) | ({joined[0]} if joined[0] else set()), 0.0, None, None))
            begin.append(max(clock.values()))
            end.append(max(clock.values()))
            joined[0] = len(ops) - 1
            return joined[0]

        joined = [0]

        def dma(dst, src, sem, *after):
            return op("sp", lambda e: e.dma_start(dst, src), *after, sem=sem,
                      cost=2.0 + 128 * 4e-3 * size(dst) / 250)

        def tt(lane, o, a, b, alu, *after):
            n = size(o)
            return op(lane, lambda e: e.tensor_tensor(o, a, b, alu), *after,
                      cost=0.07 + 0.00104 * n if lane == "dve" else 0.15 + 0.0021 * n)

        def stt(o, a, s, b, alu0, alu1, *after):
            return op("dve", lambda e: e.scalar_tensor_tensor(o, a, s, b, alu0, alu1), *after,
                      cost=0.1 + 0.00104 * size(o))

        def ts(lane, o, a, s0, s1, alu0, alu1, *after):
            cost = 0.12 + (0.0006 if lane == "dve" else 0.00087) * size(o)
            if s1 is None:
                return op(lane, lambda e: e.tensor_scalar(o, a, s0, None, alu0), *after, cost=cost)
            return op(lane, lambda e: e.tensor_scalar(o, a, s0, s1, alu0, alu1), *after, cost=cost)

        tables_in = {"Exp": "natural_log_exp_and_others", "Ln": "natural_log_exp_and_others",
                     "Silu": "silu_and_others", "Sqrt": "sqrt_and_others"}
        table = [None]

        def act(o, a, f, *after, **kw):
            cost = 0.1 + 0.00083 * size(o) + 0.09 * len(kw)
            t = tables_in.get(f.name)
            if t not in (None, table[0]):
                table[0] = t
                cost += 1.3
            return op("act", lambda e: e.activation(o, a, f, **kw), *after, cost=cost, tab=t)

        def mm(o, w, m, start, stop, *after, signal=False, **kw):
            n = size(o)
            cost = max(0.108, n * 0.000418) if m.dtype == F32R else n * 0.00167 * (0.5 if o.shape[0] == 64 else 1)
            return op("pe", lambda e: e.matmul(o, w, m, start=start, stop=stop, **kw), *after, signal=signal,
                      cost=max(cost, 0.06))

        def transpose(o, a, *after, signal=False):
            n = a.shape[0]
            return op("pe", lambda e: e.transpose(o, a, ident[0:n, 0:n]), *after, signal=signal, cost=0.11)

        def recip(o, a, *after):
            return op("dve", lambda e: e.reciprocal(o, a), *after, cost=0.1 + 0.0062 * size(o))

        def reduce(o, a, alu, *after):
            return op("dve", lambda e: e.tensor_reduce(o, a, AX.X, alu), *after, cost=0.07 + 0.00104 * size(a))

        def schedule(dense, running, limit):
            need, stuck, moves = {}, {}, [0]

            def step(g):
                try:
                    need[g] = next(g)
                except StopIteration:
                    running.remove(g)
                    need[g] = []
                if need[g] == "held":
                    stuck[g] = moves[0]
                else:
                    moves[0] += 1

            def ready_at(g):
                return 0.0 if need[g] == "held" else ready(need[g])

            def settle(forced):
                while True:
                    for g in running:
                        need.setdefault(g, [])
                    can = [g for g in running if need[g] != "held" or stuck[g] < moves[0]]
                    due = [g for g in can if ready_at(g) <= clock["pe"] + 0.2]
                    if not due and forced and can:
                        due = [min(can, key=ready_at)]
                    if not due:
                        return
                    forced = forced and need[due[0]] == "held"
                    step(due[0])

            for held in dense:
                moves[0] += held != "held"
                before = moves[0]
                settle(held == "held")
                assert held != "held" or moves[0] > before
                while len(running) > limit:
                    before = moves[0]
                    settle(True)
                    if moves[0] == before:
                        break
            assert not running

        at = [(nc.sbuf_base + 31) // 32 * 32]

        def sb(name, shape, dt=F32, offset=None):
            size = 4 * int(np.prod(shape[1:]))
            size = (size + 31) // 32 * 32
            if offset is None:
                offset = at[0]
                at[0] += size
            assert at[0] <= nc.sbuf_usable_end, (name, at[0])
            return nc.alloc_sbuf_tensor_at("s_" + name, shape, dt, offset=offset)

        x = sb("x", [128, KT, T])
        a0h = sb("a0h", [128, KT, T], F32R)
        a0l = sb("a0l", [128, KT, T], F32R)
        NRAW, NCV = 4, 4
        raw = sb("raw", [128, NRAW, 1024])
        wh = sb("wh", [128, NCV, 1024], F32R)
        wl = sb("wl", [128, NCV, 1024], F32R)
        ps = ctx.enter_context(nc.psum_tensor("ps", [128, 8, T], F32))
        ones = sb("ones", [128, 128])
        headones = sb("headones", [128, 128])
        ident = sb("ident", [128, 128])
        gains = sb("gains", [128, 7, KT])
        gn_g = sb("gn_g", [128, 4])
        eps = sb("eps", [128, 2])
        ssum = sb("ssum", [128, T])
        rstd = sb("rstd", [128, T])
        rstd_t = sb("rstd_t", [128, 8])
        small = sb("small", [128, 16, 16])
        c_act = sb("c_act", [128, KT])
        b_mod = sb("b_mod", [128, 2, 6, KT])
        mod = sb("mod", [128, 2, 6, KT])
        norm_g = sb("norm_g", [128, 2, 2, KT])
        one = sb("one", [128, 2])
        nsm = sb("nsm", [128, 292])
        ssum2 = sb("ssum2", [128, T])
        slots_at = at[0]
        hh = sb("hh", [128, KT, T], F32R)
        hl = sb("hl", [128, KT, T], F32R)
        a1h = sb("a1h", [128, KT, T], F32R)
        a1l = sb("a1l", [128, KT, T], F32R)
        ahl = ((a0h, a0l), (a1h, a1l))
        NTMP = 32 + (nc.sbuf_usable_end - at[0]) // (4 * T)
        tmp = sb("tmp", [128, NTMP, T], offset=slots_at)

        banks = [(i, None) for i in range(8)]
        tmps = [(i, None) for i in range(32, NTMP)]
        smalls = [(i, None) for i in range(16)]

        def get(pool):
            for n, (_, tok) in enumerate(pool):
                if tok is None or ready(tok) <= clock["pe"]:
                    return pool.pop(n)
            return pool.pop(min(range(len(pool)), key=lambda n: ready(pool[n][1])))

        def soon(pool, n):
            return [tok for _, tok in sorted(pool, key=lambda z: ready(z[1]))[:n]]

        def put(pool, i, *tok):
            pool.append((i, list(tok)))

        def give_back():
            tmps[:] = [(i, tok) for i, tok in tmps if i >= 32]
            h_free[0] = a_free[1] = all_done()

        def lend_h():
            for i in range(16):
                put(tmps, i, h_free[0])

        def f32(ap):
            return ap.bitcast(F32)

        def B(i):
            return ps[:, i, :]

        def S(i):
            return tmp[:, i, :]

        order = []
        ffn_parts = (8, 8, 6)

        def plan_ffn(win, wout):
            def g(p):
                for t in range(ffn_parts[p]):
                    for s in range(2):
                        order.append((win[(sum(ffn_parts[:p]) + t) * 2 + s], 1024))

            def o(p):
                k0 = sum(ffn_parts[:p])
                for d in range(8):
                    order.append((wout[d, :, k0 * 128:(k0 + ffn_parts[p]) * 128], ffn_parts[p] * 128))
            g(0), g(1), o(0), g(2), o(1), o(2)

        def plan_units(ap, n):
            for i in range(n):
                order.append((ap[i], 1024))

        def plan_out(ap, halves):
            for k in halves:
                for d in range(KT):
                    order.append((ap[d, :, k * 128:(k + 4) * 128], 512))

        plan_ffn(ins["f1i"][0], ins["f1o"][0])
        plan_units(ins["hyb"], 28)
        plan_out(ins["hybo"], [4, 0])
        plan_ffn(ins["f2i"][0], ins["f2o"][0])
        plan_ffn(ins["f1i"][1], ins["f1o"][1])
        plan_units(ins["sb"], 24)
        plan_out(ins["sbo"], [0, 4])
        plan_ffn(ins["f2i"][1], ins["f2o"][1])
        for l in range(2):
            plan_units(ins["nsa"][l], 6)
            order.append((ins["gates"][l], 320))
            plan_units(ins["nsa"][l, 6:], 8)
            plan_out(ins["mixo"][l], [0, 4])

            def ff_g(p):
                for t in range(8):
                    order.append((ins["ff1"][l, 8 * p + t], 1024))

            def ff_o(p):
                for d in range(8):
                    order.append((ins["ff2"][l, d, :, p * 1024:(p + 1) * 1024], 1024))
            ff_g(0), ff_g(1), ff_o(0), ff_g(2), ff_o(1), ff_g(3), ff_o(2), ff_o(3)

        raw_free = [None] * NRAW
        cv_free = [None] * NCV
        state = {"dma": 0, "cv": 0, "take": 0, "done": 0}
        raw_tok = {}
        cv_tok = {}

        def load_to(n):
            while state["dma"] < min(n, len(order)):
                i = state["dma"]
                src, size = order[i]
                r = i % NRAW
                raw_tok[i] = dma(raw[:, r, 0:size], src, f"raw{r}", raw_free[r])
                state["dma"] += 1

        def convert_to(n):
            while state["cv"] < min(n, len(order)):
                i = state["cv"]
                load_to(i + 1)
                src, size = order[i]
                r, c = i % NRAW, i % NCV
                hi = act(wh[:, c, 0:size], raw[:, r, 0:size], ACT.Copy, raw_tok[i], cv_free[c])
                lo = tt("dve", wl[:, c, 0:size], raw[:, r, 0:size], f32(wh[:, c, 0:size]), ALU.subtract, hi)
                cv_tok[i] = (hi, lo)
                raw_free[r] = lo
                state["cv"] += 1
                load_to(i + NRAW + 1)

        def take():
            i = state["take"]
            state["take"] += 1
            convert_to(state["done"] + NCV)
            return i

        def release(i, tok):
            cv_free[i % NCV] = tok
            state["done"] = i + 1

        def unit_mm(bank, wi, mov, ks, start, stop, *after, at=0):
            c = wi % NCV
            hi, lo = cv_tok[wi]
            tok = None
            for n, k in enumerate(ks):
                mh, ml, mt = mov[k]
                w_h = wh[:, c, (k - at) * 128:(k - at + 1) * 128]
                w_l = wl[:, c, (k - at) * 128:(k - at + 1) * 128]
                first, last = start and n == 0, stop and n == len(ks) - 1
                mm(B(bank), w_h, mh, first, False, mt, hi, *after)
                mm(B(bank), w_h, ml, False, False)
                tok = mm(B(bank), w_l, mh, False, last, lo, signal=last)
            return tok

        def tokens_mm(bks, mov, *after):
            for u in range(4):
                wi = take()
                c = wi % NCV
                hi, lo = cv_tok[wi]
                for k in (2 * u, 2 * u + 1):
                    mh, ml, mt = mov[k]
                    w_h = wh[:, c, (k % 2) * T:(k % 2 + 1) * T]
                    w_l = wl[:, c, (k % 2) * T:(k % 2 + 1) * T]
                    for t in range(4):
                        sl = slice(t * 128, (t + 1) * 128)
                        last = k == KT - 1
                        mm(B(bks[t]), mh[:, sl], w_h, k == 0, False, mt, hi, *after)
                        mm(B(bks[t]), ml[:, sl], w_h, False, False)
                        m = mm(B(bks[t]), mh[:, sl], w_l, False, last, lo, signal=last or t == 3)
                release(wi, m)
                yield m

        xt = [None] * KT
        xr = [None] * KT
        h_tok = [None] * KT
        h_free = [None]
        sum_tok = [None]
        sum_free = [None]
        rstd_tok = [None]
        rstd_t_tok = [None]
        late = [[], []]
        rstd_free = [[]]
        rstd_t_free = [[]]

        def norm_tile(d, g):
            i, free = get(tmps)
            sq = act(S(i), x[:, d, :], ACT.Square, xt[d], free)
            if d == 0:
                a = ts("pool", ssum[:, :], S(i), 1.0, 1.0, ALU.mult, ALU.mult, sq, sum_free[0])
            else:
                a = tt("pool", ssum[:, :], ssum[:, :], S(i), ALU.add, sq, sum_tok[0])
            put(tmps, i, a)
            sum_tok[0] = a
            hi = act(hh[:, d, :], x[:, d, :], ACT.Copy, h_free[0], xt[d], scale=gains[:, g, d:d + 1])
            lo = stt(hl[:, d, :], x[:, d, :], gains[:, g, d:d + 1], f32(hh[:, d, :]), ALU.mult, ALU.subtract, hi, xt[d])
            h_tok[d] = [hi, lo]
            xr[d] = [hi, lo]

        def mean_square(total, tok, freed, more):
            b, free = get(banks)
            m = mm(B(b), ones[:, :], total[:, :], True, not more, tok[0], free, const_tok, signal=True)
            freed[0] = m
            while more:
                i, sq = more.pop(0)
                m = mm(B(b), ones[:, :], S(i), False, not more, sq)
                put(tmps, i, m)
            return b, m

        def add_square(i, sq, d, total, tok, freed, more):
            if d >= KT - 2:
                more.append((i, sq))
                return
            if d == 0:
                a = ts("pool", total[:, :], S(i), 1.0, 1.0, ALU.mult, ALU.mult, sq, freed[0])
            else:
                a = tt("pool", total[:, :], total[:, :], S(i), ALU.add, sq, tok[0])
            put(tmps, i, a)
            tok[0] = a

        def norm_finish(power=False):
            b, m = mean_square(ssum, sum_tok, sum_free, late[0])
            i, ifree = get(tmps)
            if power:
                s = act(S(i), B(b), ACT.Ln, m, ifree, bias=eps[:, 0:1])
                put(banks, b, s)
                rstd_tok[0] = act(rstd[:, :], S(i), ACT.Exp, s, rstd_free[0], scale=-0.5)
                rstd_free[0] = []
                put(tmps, i, rstd_tok[0])
                return
            s = act(S(i), B(b), ACT.Sqrt, m, ifree, bias=eps[:, 0:1])
            put(banks, b, s)
            rstd_tok[0] = recip(rstd[:, :], S(i), s, rstd_free[0])
            rstd_free[0] = []
            put(tmps, i, rstd_tok[0])

        def norm_finish_tokens():
            b, free = get(banks)
            for t in range(4):
                m = mm(ps[:, b, 2 * t:2 * t + 2], ssum[:, t * 128:(t + 1) * 128], ones[:, 0:2], True, True,
                       sum_tok[0], free, signal=True)
            sum_free[0] = m
            s = act(rstd_t[:, :], ps[:, b, 0:8], ACT.Sqrt, m, rstd_t_tok[0], rstd_t_free[0], bias=eps[:, 0:1])
            put(banks, b, s)
            rstd_t_tok[0] = recip(rstd_t[:, :], rstd_t[:, :], s)
            rstd_t_free[0] = []

        def h_mov():
            return [(hh[:, k, :], hl[:, k, :], h_tok[k]) for k in range(KT)]

        a_tok = [[None] * KT, [None] * KT]
        a_free = [None, None]

        def swiglu(next_norm):
            def gate_up(p):
                ah, al = ahl[p % 2]
                for t in range(ffn_parts[p]):
                    first = p == 0 and t == 0
                    bg, fg = get(banks)
                    bu, fu = get(banks)
                    wg = take()
                    if first:
                        wu = take()
                        unit_mm(bg, wg, h_mov(), range(0, 6), True, False, fg)
                        unit_mm(bu, wu, h_mov(), range(0, 6), True, False, fu)
                        mg = unit_mm(bg, wg, h_mov(), range(6, 8), False, True)
                        mu = unit_mm(bu, wu, h_mov(), range(6, 8), False, True)
                        release(wg, mg)
                        release(wu, mu)
                        norm_finish()
                    else:
                        mg = unit_mm(bg, wg, h_mov(), range(8), True, True, fg)
                        release(wg, mg)
                        wu = take()
                        mu = unit_mm(bu, wu, h_mov(), range(8), True, True, fu)
                        release(wu, mu)
                    h_free[0] = mu
                    i, fi = get(tmps)
                    j, fj = get(tmps)
                    g = tt("dve", S(i), B(bg), rstd[:, :], ALU.mult, mg, rstd_tok[0], fi)
                    put(banks, bg, g)
                    u = tt("dve", S(j), B(bu), rstd[:, :], ALU.mult, mu, rstd_tok[0], fj)
                    put(banks, bu, u)
                    rstd_free[0] += [g, u]
                    s = act(S(i), S(i), ACT.Silu, g)
                    a = tt("pool", S(j), S(i), S(j), ALU.mult, s, u)
                    put(tmps, i, a)
                    hi = act(ah[:, t, :], S(j), ACT.Copy, a, a_free[p % 2])
                    lo = tt("dve", al[:, t, :], S(j), f32(ah[:, t, :]), ALU.subtract, hi)
                    put(tmps, j, lo)
                    a_tok[p % 2][t] = [hi, lo]
                    back()

            def down(p, last):
                nk = ffn_parts[p]
                ah, al = ahl[p % 2]
                mov = [(ah[:, k, :], al[:, k, :], a_tok[p % 2][k]) for k in range(nk)]
                for d in range(KT):
                    b, free = get(banks)
                    wi = take()
                    m = unit_mm(b, wi, mov, range(nk), True, True, free)
                    release(wi, m)
                    xt[d] = stt(x[:, d, :], B(b), 0.5, x[:, d, :], ALU.mult, ALU.add, m, xt[d], xr[d])
                    put(banks, b, xt[d])
                    if last:
                        if next_norm == "final":
                            final_norm_tile(d)
                        else:
                            norm_tile(d, next_norm)
                    back()
                    back()
                a_free[p % 2] = m

            background[1] = 0
            gate_up(0)
            gate_up(1)
            down(0, False)
            gate_up(2)
            down(1, False)
            down(2, True)
            assert background[1] == 6

        def out_proj(korder, scale, next_norm):
            def mov(ks):
                while any(a_tok[0][k] is None for k in ks):
                    yield "held"
                return [(a0h[:, k, :], a0l[:, k, :], a_tok[0][k]) for k in range(KT)]

            for half in range(2):
                ks = korder[4 * half:4 * half + 4]
                held = []

                def finish(d, b, m):
                    xt[d] = stt(x[:, d, :], B(b), scale(d), x[:, d, :], ALU.mult, ALU.add, m, xt[d], xr[d])
                    put(banks, b, xt[d])
                    if half == 0:
                        return
                    if next_norm == "sum":
                        sum_tile(d)
                    else:
                        norm_tile(d, next_norm)

                for d in range(KT):
                    b = None
                    if half and d < 3:
                        mv = yield from mov(ks[:-1])
                        b, free = get(banks)
                        wi = take()
                        unit_mm(b, wi, mv, ks[:-1], True, False, free, at=ks[0])
                        held.append((d, b, wi))
                        yield
                    if half and d < 2:
                        continue
                    mv = yield from mov(ks)
                    for e, b, wi in held:
                        m = unit_mm(b, wi, mv, ks[-1:], False, True, at=ks[0])
                        release(wi, m)
                        finish(e, b, m)
                    if held:
                        held = []
                        yield
                        continue
                    b, free = get(banks)
                    wi = take()
                    m = unit_mm(b, wi, mv, ks, True, True, free, at=ks[0])
                    release(wi, m)
                    finish(d, b, m)
                    yield
            a_free[0] = m

        def at_block(three, j):
            return three[(0, 1, 2, 1)[j]], (0, 0, 0, 384)[j], T - 128 * j

        def project(n=KT):
            b, free = get(banks)
            wi = take()
            m = unit_mm(b, wi, h_mov(), range(n), True, True, free)
            h_free[0] = m
            release(wi, m)
            return b, m

        def rope(bm, o, ofree, cr, sr, tabs_t, mask):
            bank, m = bm
            j, jfree = get(tmps)
            t1 = tt("dve", S(o), B(bank), cr, ALU.mult, m, tabs_t, ofree)
            sh = op("dve", lambda e: e.stream_shuffle(S(j), B(bank), mask), m, jfree, cost=0.6)
            put(banks, bank, t1, sh)
            s2 = tt("pool", S(j), S(j), sr, ALU.mult, sh, tabs_t)
            r = tt("pool", S(o), S(o), S(j), ALU.add, s2, t1)
            put(tmps, j, r)
            return r

        def get3(pool):
            got = [get(pool) for _ in range(3)]
            return [i for i, _ in got], [tok for _, tok in got]

        def softmax_scores(q, k, bias, sts, *after):
            zs, zfree = [], []
            for hd in range(2):
                z, f = get3(tmps)
                zs.append(z)
                zfree.append(f)
            e_tok = [[None] * 4 for _ in range(2)]
            for group in ((3,), (2, 0), (1,)):
                if group[0] != 3:
                    yield [after, soon(banks, 2)]
                bs = [get(banks) for _ in range(2)]
                reads = [[], []]
                for t in group:
                    n = (t + 1) * 128
                    c = at_block((0, 0, 0), 3 - t)[1]
                    for hd in range(2):
                        m = mm(ps[:, bs[hd][0], c:c + n], q[hd][:, t * 128:(t + 1) * 128], k[hd][:, 0:n], True, True,
                               after, bs[hd][1], signal=t == group[-1])
                for t in group:
                    n = (t + 1) * 128
                    for hd in range(2):
                        z, c, _ = at_block(zs[hd], 3 - t)
                        zt, mn = tmp[:, z, c:c + n], sts[hd][:, t:t + 1]
                        r = op("dve", lambda e, o=zt, s=ps[:, bs[hd][0], c:c + n], bi=bias[:, T - n:T], mn=mn: e.tensor_tensor_reduce(
                            out=o, in0=s, in1=bi, scale=-0.125, scalar=1e30, op0=ALU.add, op1=ALU.min, accum_out=mn),
                            m, zfree[hd], cost=0.1 + 0.00104 * n)
                        reads[hd].append(r)
                        e_tok[hd][t] = act(zt, zt, ACT.Exp, r, scale=-1.0, bias=mn, accum_out=sts[hd][:, 4 + t:5 + t])
                for hd in range(2):
                    put(banks, bs[hd][0], reads[hd])
            return zs, e_tok, m

        def softmax_scale(zs, scale, r):
            tok = [None] * 4
            for t in (3, 2, 1, 0):
                z, c, n = at_block(zs, 3 - t)
                tok[t] = ts("dve", tmp[:, z, c:c + n], tmp[:, z, c:c + n], scale[t], None, ALU.mult, None, r)
            return tok

        def transposed(zs, p_tok, lane="act"):
            bs, bfree = get3(banks)
            ts_, tfree = get3(tmps)
            done = []
            for kts in ((0,), (1, 3), (2,)):
                for kt in kts:
                    b, c, _ = at_block(bs, kt)
                    for t in range(kt, 4):
                        z, cz, _ = at_block(zs, 3 - t)
                        m = transpose(ps[:, b, c + (t - kt) * 128:c + (t - kt + 1) * 128],
                                      tmp[:, z, cz + kt * 128:cz + (kt + 1) * 128], p_tok[t], bfree, signal=t == 3)
                i = kts[0]
                n = 512 if i < 2 else 256
                if lane == "act":
                    e = act(tmp[:, ts_[i], 0:n], ps[:, bs[i], 0:n], ACT.Copy, m, tfree)
                else:
                    e = ts("dve", tmp[:, ts_[i], 0:n], ps[:, bs[i], 0:n], 1.0, None, ALU.mult, None, m, tfree)
                put(banks, bs[i], e)
                done.append(e)
            for z in zs:
                put(tmps, z, m)
            return ts_, done

        def values(o, ofree, parts, first, last):
            for kt in range(4):
                for hd in range(2):
                    slots, toks, v, vt = parts[hd]
                    z, c, n = at_block(slots, kt)
                    m = mm(ps[64 * hd:64 * hd + 64, o, kt * 128:T], v(kt), tmp[:, z, c:c + n],
                           first and kt == 0, last and kt == 3, toks, vt, ofree, signal=kt == 3)
            for slots, _, _, _ in parts:
                for z in slots:
                    put(tmps, z, m)
            return m

        def to_mix(slot, o, m):
            hi = act(a0h[:, slot, :], B(o), ACT.Copy, m, a_free[0])
            lo = tt("dve", a0l[:, slot, :], B(o), f32(a0h[:, slot, :]), ALU.subtract, hi)
            put(banks, o, lo)
            a_tok[0][slot] = [hi, lo]

        def v_units(units, h, each):
            bs = [get(banks) for _ in range(4)]
            for m in tokens_mm([b for b, _ in bs], h, [f for _, f in bs]):
                yield
            h_free[0] = m
            units()
            for t in range(4):
                each(t, bs[t][0], m)

        def hyb(next_norm):
            vr, vd, sg, tabs = (tmp[:, 4 * i:4 * i + 4, :] for i in range(4, 8))
            scratch_free = a_free[1]
            shuf_r = [(i + 16) % 32 for i in range(32)]
            shuf_d = [(i + 8) % 16 if i < 16 else i for i in range(32)]
            bias, bfree = get(tmps)
            tab_t = dma(tabs[:, :, :], ins["rope"], "tab0", scratch_free)
            bias_t = dma(S(bias), ins["dilbias"], "tab1", bfree)
            rt, vd_tok, vr_tok, sg_tok = [None] * 4, [None] * 4, [None] * 4, [None] * 4
            a_tok[0] = [None] * KT

            def finish_norm():
                norm_finish()
                norm_finish_tokens()
                for i in (2, 3, 0, 1):
                    rt[i] = tt("pool", tabs[:, i, :], tabs[:, i, :], rstd[:, :], ALU.mult, tab_t, rstd_tok[0])
                rstd_free[0] += rt

            def take_vd(t, b, m):
                vd_tok[t] = act(vd[:, t, :], B(b), ACT.Copy, m, rstd_t_tok[0], scratch_free,
                                scale=rstd_t[:, 2 * t:2 * t + 1])
                put(banks, b, vd_tok[t])
                rstd_t_free[0].append(vd_tok[t])

            def take_vr(t, b, m):
                e = act(vr[:, t, :], B(b), ACT.Copy, m, rstd_t_tok[0], scratch_free, scale=rstd_t[:, 2 * t:2 * t + 1])
                put(banks, b, e)
                rstd_t_free[0].append(e)
                k, kfree = get(smalls)
                v3 = vr[:, t, :].rearrange("p (h d) -> p h d", d=64)
                mu = small[:, k, 0:8]
                r = reduce(mu, v3, ALU.add, e, kfree)
                r = ts("dve", mu, mu, 1.0 / 64, None, ALU.mult, None, r)
                vr_tok[t] = tt("dve", v3, v3, mu.unsqueeze(2).to_broadcast([128, 8, 64]), ALU.subtract, r)
                put(smalls, k, vr_tok[t])

            def dilated(pr, bq, bk):
                (q, qf), (k, kf) = get(tmps), get(tmps)
                qt = rope(bq, q, qf, tabs[:, 2, :], tabs[:, 3, :], [rt[2], rt[3]], shuf_d)
                kt_ = rope(bk, k, kf, tabs[:, 2, :], tabs[:, 3, :], [rt[2], rt[3]], shuf_d)
                yield [qt, kt_]
                st, stfree = get(smalls)
                e = []
                halves = slice(0, 64), slice(64, 128)
                z, et, m = yield from softmax_scores([tmp[r, q, :] for r in halves], [tmp[r, k, :] for r in halves], S(bias),
                                                     [small[:, st, 8 * hd:8 * hd + 8] for hd in range(2)], qt, kt_, bias_t, stfree)
                for hd in range(2):
                    den = small[:, st, 8 * hd + 4:8 * hd + 8]
                    r = recip(den, den, et[hd])
                    e.append(softmax_scale(z[hd], [den[:, t:t + 1] for t in range(4)], r))
                put(tmps, q, m)
                put(tmps, k, m)
                put(smalls, st, e)
                parts = []
                for hd in range(2):
                    yield e[hd]
                    tz, tt_ = transposed(z[hd], e[hd])
                    col = (2 * pr + hd) * 64
                    parts.append((tz, tt_, lambda kt, col=col: vd[:, kt, col:col + 64], vd_tok))
                yield [parts[0][1], parts[1][1]]
                o, of = get(banks)
                m = values(o, of, parts, True, True)
                to_mix(4 + pr, o, m)

            def retention(pr, bq, bk):
                (q, qf), (k, kf) = get(tmps), get(tmps)
                qt = rope(bq, q, qf, tabs[:, 0, :], tabs[:, 1, :], [rt[0], rt[1]], shuf_r)
                kt_ = rope(bk, k, kf, tabs[:, 0, :], tabs[:, 1, :], [rt[0], rt[1]], shuf_r)
                dec = []
                for hd in range(2):
                    i, f = get(tmps)
                    dec.append((i, dma(S(i), ins["decay"][2 * pr + hd], f"dec{2 * pr + hd}", f)))
                yield [qt, kt_]
                zs, zf, toks = [], [], [[], []]
                for hd in range(2):
                    z, f = get3(tmps)
                    zs.append(z)
                    zf.append(f)
                for js in ((0,), (1, 3), (2,)):
                    if js[0]:
                        yield [soon(banks, 2)]
                    bs = [get(banks) for _ in range(2)]
                    reads = [[], []]
                    for j in js:
                        _, c, n = at_block(zs[0], j)
                        for hd in range(2):
                            rows = slice(64 * hd, 64 * hd + 64)
                            m = mm(ps[:, bs[hd][0], c:c + n], tmp[rows, k, j * 128:(j + 1) * 128], tmp[rows, q, j * 128:T], True, True,
                                   qt, kt_, bs[hd][1], signal=j == js[-1])
                    for j in js:
                        for hd in range(2):
                            z, c, n = at_block(zs[hd], j)
                            reads[hd].append(tt("dve", tmp[:, z, c:c + n], ps[:, bs[hd][0], c:c + n], S(dec[hd][0])[:, 0:n],
                                                ALU.mult, m, zf[hd], dec[hd][1]))
                    for hd in range(2):
                        put(banks, bs[hd][0], reads[hd])
                        toks[hd] += reads[hd]
                parts = []
                for hd in range(2):
                    put(tmps, dec[hd][0], toks[hd])
                    col = (2 * pr + hd) * 64
                    parts.append((zs[hd], toks[hd], lambda kt, col=col: vr[:, kt, col:col + 64], vr_tok))
                put(tmps, q, m)
                put(tmps, k, m)
                yield [parts[0][1], parts[1][1]]
                o, of = get(banks)
                m = values(o, of, parts, True, True)
                i, f = get(tmps)
                sq = act(S(i), B(o), ACT.Square, m, f)
                yield [sq]
                vb, vf = get(banks)
                m2 = mm(B(vb), headones[:, :], S(i), True, True, sq, vf, signal=True)
                s = act(S(i), B(vb), ACT.Sqrt, m2, bias=eps[:, 1:2])
                put(banks, vb, s)
                r = recip(S(i), S(i), s)
                y = tt("dve", S(i), B(o), S(i), ALU.mult, r, m)
                put(banks, o, y)
                while sg_tok[pr] is None:
                    yield "held"
                y = stt(S(i), S(i), gn_g[:, pr:pr + 1], sg[:, pr, :], ALU.mult, ALU.mult, y, sg_tok[pr])
                hi = act(a0h[:, pr, :], S(i), ACT.Copy, y, a_free[0])
                lo = tt("dve", a0l[:, pr, :], S(i), f32(a0h[:, pr, :]), ALU.subtract, hi)
                put(tmps, i, lo)
                a_tok[0][pr] = [hi, lo]

            running = []

            def dense():
                yield from v_units(finish_norm, h_mov(), take_vd)
                yield from v_units(lambda: None, h_mov(), take_vr)
                for kind, pr in HYB_ORDER:
                    if kind == "g":
                        b, m = project()
                        g = tt("dve", sg[:, pr, :], B(b), rstd[:, :], ALU.mult, m, rstd_tok[0], scratch_free)
                        put(banks, b, g)
                        rstd_free[0].append(g)
                        sg_tok[pr] = act(sg[:, pr, :], sg[:, pr, :], ACT.Silu, g)
                        yield
                        continue
                    q = project()
                    yield
                    k = project()
                    running.append((dilated if kind == "d" else retention)(pr, q, k))
                    yield
                lend_h()
                yield from out_proj([4, 5, 6, 7, 0, 1, 2, 3], lambda d: 1.0, next_norm)

            schedule(dense(), running, 2)
            put(tmps, bias, all_done())
            give_back()

        def stick(next_norm):
            vs = tmp[:, 16:24, :].rearrange("p (t a) d -> p t (a d)", a=2)
            masks = sb("sbmask", [128, 2, 128], mybir.dt.bfloat16, offset=slots_at + 24 * 2048)
            scratch_free = a_free[1]
            mi, mf = get(tmps)
            mask_t = dma(tmp[:, mi, 0:256], ins["sbmask"], "tab0", mf)
            mask_t = op("dve", lambda e: e.tensor_copy(masks[:, :, :].rearrange("p a b -> p (a b)"), tmp[:, mi, 0:256]), mask_t,
                        scratch_free)
            put(tmps, mi, mask_t)
            for i in range(25, 32):
                put(tmps, i, scratch_free)
            v_tok = [[None] * 4, [None] * 4]
            a_tok[0] = [None] * KT

            def take_v(half):
                def each(t, b, m):
                    v_tok[half][t] = act(vs[:, t, half * T:(half + 1) * T], B(b), ACT.Copy, m, rstd_t_tok[0], scratch_free,
                                         scale=rstd_t[:, 2 * t:2 * t + 1])
                    put(banks, b, v_tok[half][t])
                    rstd_t_free[0].append(v_tok[half][t])
                return each

            def finish_norm():
                norm_finish()
                norm_finish_tokens()

            def head_pair(pr, bq, bk):
                (q, qf), (k, kf) = get(tmps), get(tmps)
                qt = stt(S(q), B(bq[0]), 0.125, rstd[:, :], ALU.mult, ALU.mult, bq[1], qf, rstd_tok[0])
                kt_ = tt("dve", S(k), B(bk[0]), rstd[:, :], ALU.mult, bk[1], kf, rstd_tok[0])
                put(banks, bq[0], qt)
                put(banks, bk[0], kt_)
                rstd_free[0] += [qt, kt_]
                yield [qt, kt_]
                zs, zf, e_tok = [], [], [[None] * 4 for _ in range(2)]
                for hd in range(2):
                    z, f = get3(tmps)
                    zs.append(z)
                    zf.append(f)
                for group in ((3,), (2, 0), (1,)):
                    if group[0] != 3:
                        yield [soon(banks, 2)]
                    bs = [get(banks) for _ in range(2)]
                    for t in group:
                        n = (t + 1) * 128
                        c = at_block(zs[0], 3 - t)[1]
                        for hd in range(2):
                            rows = slice(64 * hd, 64 * hd + 64)
                            mm(ps[:, bs[hd][0], c:c + n], tmp[rows, q, t * 128:(t + 1) * 128], tmp[rows, k, 0:n], t != 0, False,
                               qt, kt_, bs[hd][1], skip_group_check=True)
                    for t in group:
                        c = at_block(zs[0], 3 - t)[1] + t * 128
                        for hd in range(2):
                            m = mm(ps[:, bs[hd][0], c:c + 128], masks[:, 1, :], masks[:, 0, :], False, t == group[-1], mask_t,
                                   signal=True, skip_group_check=True)
                    w = 512 if group[0] > 1 else 256
                    for hd in range(2):
                        zb = ps[:, bs[hd][0], 0:w]
                        l, lf = get(tmps)
                        li, si = tmp[:, l, 0:w], tmp[:, at_block(zs[hd], 3 - group[0])[0], 0:w]
                        r = act(li, zb, ACT.Abs, m, lf)
                        r = act(li, li, ACT.Exp, r, scale=-1.0)
                        r = act(li, li, ACT.Ln, r, bias=1.0)
                        r = stt(si, zb, 0.0, li, ALU.max, ALU.add, r, zf[hd])
                        put(tmps, l, r)
                        sums = []
                        for t in group:
                            z, c, _ = at_block(zs[hd], 3 - t)
                            n = (t + 1) * 128
                            back_to_front = tmp[:, z, c:c + n][:, ::-1]
                            sums.append(op("dve", lambda e, o=back_to_front, n=n: e.tensor_tensor_scan(
                                o, one[:, 0:1].to_broadcast([128, n]), o, 0.0, ALU.mult, ALU.add), r, const_tok, cost=0.1 + 0.00104 * n))
                        r = tt("dve", si, zb, si, ALU.subtract, sums)
                        put(banks, bs[hd][0], r)
                        r = act(si, si, ACT.Exp, r)
                        for t in group:
                            e_tok[hd][t] = r
                put(tmps, q, m)
                put(tmps, k, m)
                parts = []
                for hd in range(2):
                    yield e_tok[hd]
                    tz, tt_ = transposed(zs[hd], e_tok[hd], "act" if hd else "dve")
                    col = (2 * pr + hd) * 64
                    parts.append((tz, tt_, lambda kt, col=col: vs[:, kt, col:col + 64], v_tok[pr // 4]))
                yield [parts[0][1], parts[1][1]]
                o, of = get(banks)
                m = values(o, of, parts, True, True)
                to_mix(pr, o, m)

            running = []

            def dense():
                yield from v_units(finish_norm, h_mov(), take_v(0))
                yield from v_units(lambda: None, h_mov(), take_v(1))
                for pr in range(8):
                    q = project()
                    yield
                    k = project()
                    running.append(head_pair(pr, q, k))
                    yield
                lend_h()
                yield from out_proj(list(range(8)), lambda d: 1.0, next_norm)

            schedule(dense(), running, 1)
            give_back()

        mod_tok = [[[] for _ in range(6)] for _ in range(2)]

        def modulation():
            silu_tok = act(c_act[:, :], c_act[:, :], ACT.Silu, const_tok)
            for l in range(2):
                for c in range(12):
                    acc, acc_f = get(tmps)
                    w = [get(tmps) for _ in range(2)]
                    w_free = [f for _, f in w]

                    def load(k):
                        i = k % 2
                        return dma(S(w[i][0]), ins["w_mod"][l, k * 128:(k + 1) * 128, c * T:(c + 1) * T], f"wm{2 * (c % 2) + i}", w_free[i])
                    tok = [load(0), load(1)]
                    yield
                    a = None
                    for k in range(KT):
                        i = k % 2
                        if k == 0:
                            a = ts("dve", S(acc), S(w[i][0]), c_act[:, 0:1], None, ALU.mult, None, tok[i], silu_tok, acc_f)
                        else:
                            a = stt(S(acc), S(w[i][0]), c_act[:, k:k + 1], S(acc), ALU.mult, ALU.add, tok[i], silu_tok, a)
                        w_free[i] = a
                        if k + 2 < KT:
                            tok[i] = load(k + 2)
                        yield
                    yield
                    b, f = get(banks)
                    for d in range(4):
                        m = mm(ps[:, b, 2 * d:2 * d + 2], tmp[:, acc, d * 128:(d + 1) * 128], one[:, :], True, True, a, f,
                               signal=True)
                    put(tmps, acc, m)
                    for i in range(2):
                        put(tmps, w[i][0], w_free[i])
                    v = ps[:, b, 0:8].rearrange("p (d t) -> p d t", t=2)[:, :, 0]
                    o, ds = c // 2, slice(4 * (c % 2), 4 * (c % 2) + 4)
                    r = tt("dve", mod[:, l, o, ds], v, b_mod[:, l, o, ds], ALU.add, m, const_tok)
                    put(banks, b, r)
                    if o in (1, 4):
                        r = stt(mod[:, l, o, ds], mod[:, l, o, ds], 1.0, norm_g[:, l, o // 3, ds], ALU.add, ALU.mult, r)
                    mod_tok[l][o].append(r)
                    yield "whole"

        background = [None, 0]

        def back():
            if background[1] < 6 and next(background[0], "whole") == "whole":
                background[1] += 1

        def sum_tile(d):
            i, free = get(tmps) if d < KT - 2 else tmps.pop([i >= 32 for i, _ in tmps].index(True))
            sq = act(S(i), x[:, d, :], ACT.Square, xt[d], free)
            xr[d] = [sq]
            add_square(i, sq, d, ssum, sum_tok, sum_free, late[0])

        def modulated(l, half, gain=None):
            g, s_ = mod[:, l, 3 * half + 1, :], mod[:, l, 3 * half, :]
            mt = [mod_tok[l][3 * half + 1], mod_tok[l][3 * half]]
            for d in range(KT):
                i, f = get(tmps)
                if gain is None:
                    r = tt("dve", S(i), x[:, d, :], rstd[:, :], ALU.mult, xt[d], rstd_tok[0], f)
                else:
                    r = stt(S(i), x[:, d, :], gain[:, d:d + 1], rstd[:, :], ALU.mult, ALU.mult, xt[d], rstd_tok[0], f)
                xr[d] = [xr[d], r]
                rstd_free[0].append(r)
                hi = act(hh[:, d, :], S(i), ACT.Identity, r, h_free[0], mt, scale=g[:, d:d + 1], bias=s_[:, d:d + 1])
                r = ts("dve", S(i), S(i), g[:, d:d + 1], s_[:, d:d + 1], ALU.mult, ALU.add, r, mt, hi)
                lo = tt("dve", hl[:, d, :], S(i), f32(hh[:, d, :]), ALU.subtract, r)
                put(tmps, i, lo)
                h_tok[d] = [hi, lo]

        def final_norm_tile(d):
            sum_tile(d)
            i, free = get(tmps)
            sq = act(S(i), x[:, d, :], ACT.Square, xt[d], free, scale=gains[:, 6, d:d + 1])
            xr[d] = [xr[d], sq]
            add_square(i, sq, d, ssum2, sum2_tok, sum2_free, late[1])

        sum2_tok, sum2_free = [None], [None]

        def final_norm_finish():
            b2, m2 = mean_square(ssum2, sum2_tok, sum2_free, late[1])
            norm_finish(True)
            first = ssum2[:, :]
            r = tt("dve", first, rstd[:, :], rstd[:, :], ALU.mult, rstd_tok[0], m2)
            i, f = get(tmps)
            r = tt("dve", S(i), B(b2), first, ALU.mult, m2, r, f)
            put(banks, b2, r)
            k = ts("dve", first, rstd[:, :], 1.0, None, ALU.mult, None, r)
            r = act(S(i), S(i), ACT.Ln, r, bias=eps[:, 0:1])
            r = act(S(i), S(i), ACT.Exp, r, scale=-0.5)
            rstd_tok[0] = tt("dve", rstd[:, :], first, S(i), ALU.mult, r, k)
            put(tmps, i, rstd_tok[0])
            return k

        def final_norm_scale(k):
            for d in range(KT):
                xt[d] = stt(x[:, d, :], x[:, d, :], gains[:, 6, d:d + 1], ssum2[:, :], ALU.mult, ALU.mult, k, xr[d], xt[d])
                xr[d] = None

        def hybrid(l):
            qT, kT = tmp[:, 16:20, :], tmp[:, 20:22, :]
            vsw = tmp[:, 22:24, :].rearrange("p a (b c) -> p (a b) c", b=2)
            w1 = tmp[:, 24:28, :].rearrange("p (kv a) (j e) -> p kv (a j) e", kv=2, e=64)
            win = tmp[:, 28:30, :].rearrange("p a (j g n) -> p (a j) g n", g=2, n=32)
            qtab = tmp[:, 30, :].rearrange("p (a t d) -> p a t d", a=2, d=64)
            poolw = tmp[:, 31, :].rearrange("p (g d) -> p g d", g=4)
            scratch_free = a_free[1]
            small_free = [nsa_free[0]]
            a_tok[0] = [None] * KT
            st_ = scratch_free
            (rt_, rf), (g_, gf) = get(tmps), get(tmps)
            rope_t = dma(S(rt_), ins["rope2"], "tab0", rf)
            gain_t = dma(tmp[:, g_, 0:256], ins["qk_gain"][l], "tab1", gf)
            w1_t = dma(tmp[:, 24:28, :], ins["cmp_w1"][l].rearrange("p a j e -> p (a j e)").rearrange("p (s c) -> p s c", c=T), "tab2", st_)
            pw_t = dma(poolw, ins["pool_w"][l], "tab3", st_)
            sm_t = dma(nsm[:, :], ins["nsa_small"][l], "tab4", small_free)
            (mk_, mf) = get(tmps)
            mk_t = dma(S(mk_), ins["cmp_mask"], "tab5", mf)
            cmpmask = S(mk_)
            bias_, bf_ = get(tmps)
            bias_t = dma(S(bias_), ins["causal"], "tab6", bf_)
            pe, w2, pscale, ctab = nsm[:, 0:32], nsm[:, 32:96], nsm[:, 96:100], nsm[:, 100:228]
            gcos = S(rt_)[:, 0:256].rearrange("p (t d) -> p t d", d=64)
            gsin = S(rt_)[:, 256:512].rearrange("p (t d) -> p t d", d=64)

            def swapped(a):
                return a

            def gain(i):
                return tmp[:, g_, 64 * i:64 * i + 64].unsqueeze(1).to_broadcast([128, 4, 64])

            def gain_swapped(i, h):
                o_ = 64 * i + 32 * (1 - h)
                return tmp[:, g_, o_:o_ + 32].unsqueeze(1).to_broadcast([128, 4, 32])

            def make_table(dst, i, after):
                a = tt("pool", dst[:, 0, :, :], gcos, gain(i), ALU.mult, rope_t, gain_t, st_, after)
                b = [a]
                for h in range(2):
                    b += [tt("pool", dst[:, 1, :, 32 * h:32 * h + 32], gsin[:, :, 32 * h:32 * h + 32], gain_swapped(i, h),
                           ALU.mult, rope_t, gain_t, st_, after)]
                return b
            qtab_t = make_table(qtab, 0, None)
            (kt1, k1f), (kt2, k2f) = sorted((get(tmps), get(tmps)), key=lambda z: z[0])
            ktab = [S(k)[:, 0:512].rearrange("p (a t d) -> p a t d", a=2, d=64) for k in (kt1, kt2)]
            ktab_t = [make_table(ktab[0], 2, k1f), make_table(ktab[1], 3, k2f)]
            for z, t_ in ((rt_, [qtab_t, ktab_t]), (g_, [qtab_t, ktab_t])):
                put(tmps, z, t_)

            def normed(src, dst, heads, tab, tab_t, st, *after):
                k, kf = get(smalls)
                i, f = get(tmps)
                P_ = src.shape[0]
                w = heads * 64
                t = tmp[0:P_, i, 0:w].rearrange("p (h d) -> p h d", d=64)
                sq = act(t, src, ACT.Square, *after, f)
                r8 = small[0:P_, k, 0:heads]
                r = reduce(r8, t, ALU.add, sq, kf)
                r = act(r8, r8, ACT.Sqrt, r, scale=1.0 / 64, bias=eps[0:P_, 0:1])
                r = recip(r8, r8, r)
                nrm = tt("dve", t, src, r8.unsqueeze(2).to_broadcast([P_, heads, 64]), ALU.mult, r)
                put(smalls, k, nrm)
                j, jf = get(tmps)
                sn = tmp[0:P_, j, 0:w].rearrange("p (h d) -> p h d", d=64)
                def like(ap, tb):
                    return ap if len(tb.shape) == 3 else ap.rearrange("p (a h) d -> p a h d", a=tb.shape[1])
                a = [tt("dve", like(sn[:, :, 32 * h:32 * h + 32], tab(1, h)), like(t[:, :, 32 - 32 * h:64 - 32 * h], tab(1, h)),
                        tab(1, h), ALU.mult, nrm, tab_t, jf) for h in range(2)]
                c = tt("pool", like(t, tab(0, None)), like(t, tab(0, None)), tab(0, None), ALU.mult, nrm, tab_t, a)
                e = tt("pool", dst, t, sn, ALU.add, c, a)
                put(tmps, i, e)
                put(tmps, j, e)
                return nrm, e

            q_tok, k_tok, vs_tok = [None] * 4, [None] * 4, [None] * 4
            qT_tok, kT_tok = [None] * 4, [None] * 4

            def take_q(t, b, m):
                i, f = get(tmps)

                def tab(a, h):
                    z = qtab[:, a, t, :] if h is None else qtab[:, a, t, 32 * h:32 * h + 32]
                    return z.unsqueeze(1).to_broadcast([128, 8, z.shape[1]])
                bank3 = B(b).rearrange("p (h d) -> p h d", d=64)
                nrm, e = normed(bank3, S(i).rearrange("p (h d) -> p h d", d=64), 8, tab, qtab_t, None, m, f)
                put(banks, b, nrm)
                running.append(turn(t, i, e, qT, qT_tok, 4))

            def turn(t, i, e, dst, toks, n):
                yield [e]
                b, f = get(banks)
                for p in range(n):
                    m = transpose(ps[:, b, p * 128:(p + 1) * 128], tmp[:, i, p * 128:(p + 1) * 128], e, f, signal=p == n - 1)
                put(tmps, i, m)
                src = ps[:, b, 0:n * 128].rearrange("p (n t) -> p n t", t=128)
                toks[t] = act(dst[:, :, t * 128:(t + 1) * 128], src, ACT.Copy, m, st_)
                put(banks, b, toks[t])

            def take_kv(t, b, m):
                i, f = get(tmps)

                def tab(a, h):
                    z = tmp[:, kt1:kt2 + 1:kt2 - kt1, :].rearrange("p s (a t d) -> p s a t d", a=2, d=64)[:, :, a, t, :]
                    z = z if h is None else z[:, :, 32 * h:32 * h + 32]
                    return z.unsqueeze(2).to_broadcast([128, 2, 2, z.shape[2]])
                nr, e = normed(ps[:, b, 0:256].rearrange("p (h d) -> p h d", d=64),
                               tmp[:, i, 0:256].rearrange("p (h d) -> p h d", d=64), 4, tab, ktab_t, None, m, f)
                vs_tok[t] = act(vsw[:, t, :], ps[:, b, 256:512], ACT.Copy, m, nr, st_)
                put(banks, b, nr, vs_tok[t])
                running.append(turn(t, i, e, kT, kT_tok, 2))

            gate_tok = [None]
            gs, gsf = get(tmps)
            gate_t = tmp[:, gs, 0:96].rearrange("p (t b h) -> p t b h", b=3, h=8)

            def gates(b, m):
                i, f = get(tmps)
                e = act(tmp[0:32, i, :], ps[0:32, b, :], ACT.Copy, m, f)
                put(banks, b, e)
                yield [e]
                b, f = get(banks)
                for t in range(4):
                    m = transpose(ps[:, b, t * 32:(t + 1) * 32], tmp[0:32, i, t * 128:(t + 1) * 128], e, f, signal=t == 3)
                put(tmps, i, m)
                g4 = tmp[:, gs, 0:96].rearrange("p (t c) -> p t c", c=24)
                e = act(g4, ps[:, b, 0:128].rearrange("p (t c) -> p t c", c=32)[:, :, 0:24], ACT.Exp, m, gsf, scale=-1.0)
                put(banks, b, e)
                e = ts("dve", tmp[:, gs, 0:96], tmp[:, gs, 0:96], 1.0, None, ALU.add, None, e)
                gate_tok[0] = recip(tmp[:, gs, 0:96], tmp[:, gs, 0:96], e)

            vc, vcf = get(tmps)
            kcT = tmp[:, vc, 128:192]
            kz = op("pool", lambda e: e.memset(kcT, 0.0), vcf)
            vcmp = tmp[:, vc, 0:128]
            pc, pcf = [None, None], [None, None]
            for g in range(2):
                pc[g], pcf[g] = get(tmps)
            kc_tok, vc_tok, pc_tok = [None], [None], [None, None]
            sil_bank = [None, None, None]

            def windows(kv, b, m):
                toks = []
                slots = []
                for g in range(2):
                    i, f = get(tmps)
                    src = ps[64 * g:64 * g + 64, b, :]
                    e0 = act(tmp[0:64, i, :], src, ACT.Copy, m, f)
                    e1 = act(tmp[64:128, i, 0:511], src[:, 1:512], ACT.Copy, m, f)
                    w_ = tmp[:, i, :].rearrange("p (n s) -> p n s", s=16)
                    slots.append((i, w_, [e0, e1]))
                put(banks, b, [e for _, _, e in slots])
                while kv and win_free[0] is None:
                    yield "held"
                z = op("pool", lambda e: e.memset(win[:, :, :, 31:32], 0.0), st_, win_free[0])
                for g, (i, w_, e) in enumerate(slots):
                    for hf in range(2):
                        src = w_[:, hf:hf + 31, :].rearrange("p n (j two) -> p j n two", two=2)[:, :, :, 0]
                        toks.append(tt("dve", win[:, 8 * hf:8 * hf + 8, g, 0:31], src,
                                       pe[:, 16 * kv + 8 * hf:16 * kv + 8 * hf + 8].unsqueeze(2).to_broadcast([128, 8, 31]),
                                       ALU.add, e, sm_t, st_, win_free[0]))
                    put(tmps, i, toks[-2:])
                yield [toks, z, w1_t]
                if kv == 0:
                    sil_bank[0], sil_bank[1] = get(banks)
                sbk = sil_bank[0]
                for j in range(16):
                    m = mm(ps[64 * kv:64 * kv + 64, sbk, 0:64], w1[:, kv, j, :],
                           win[:, j, :, :].rearrange("p g n -> p (g n)"), j == 0, j == 15, toks, z, w1_t, sil_bank[1],
                           signal=j == 15)
                win_free[0] = m
                sl, slf = get(tmps)
                rows = slice(64 * kv, 64 * kv + 64)
                if kv == 0:
                    sil = tmp[rows, sl, 0:64]
                    e = [act(sil, ps[rows, sbk, 0:64], ACT.Silu, m, slf)]
                    sil_bank[2] = e
                else:
                    sil = tmp[rows, sl, 0:256]
                    e = []
                    for g in range(2):
                        src = ps[rows, sbk, g * 32:(g + 1) * 32].unsqueeze(1).to_broadcast([64, 4, 32])
                        e.append(act(sil[:, g * 128:(g + 1) * 128].rearrange("p (r n) -> p r n", n=32), src, ACT.Silu, m, slf))
                    put(banks, sbk, e, sil_bank[2])
                yield [e]
                b, f = get(banks)
                if kv == 0:
                    for g in range(2):
                        m = mm(ps[0:32, b, g * 64:(g + 1) * 64], sil[:, g * 32:(g + 1) * 32], w2[rows, :], True, True, e, f,
                               sm_t, signal=True)
                    put(tmps, sl, m)
                    i, f = get(tmps)

                    def tab(a, h):
                        z = ctab[0:32, 64 * a:64 * a + 64] if h is None else ctab[0:32, 64 * a + 32 * h:64 * a + 32 * h + 32]
                        return z.unsqueeze(1).to_broadcast([32, 2, z.shape[1]])
                    nrm, e = normed(ps[0:32, b, 0:128].rearrange("p (h d) -> p h d", d=64),
                                    tmp[0:32, i, 0:128].rearrange("p (h d) -> p h d", d=64), 2, tab, ctab_t, None, m, f)
                    put(banks, b, nrm)
                    yield [e]
                    b, f = get(banks)
                    m = transpose(ps[:, b, 0:32], tmp[0:32, i, 0:128], e, f, signal=True)
                    put(tmps, i, m)
                    kc = []
                    for g in range(2):
                        rows = slice(64 * g, 64 * g + 64)
                        kc.append(act(kcT[rows, 32 * g:32 * g + 32], ps[rows, b, 0:32], ACT.Copy, m, kz))
                    kc_tok[0] = kc
                    put(banks, b, kc)
                else:
                    for g in range(2):
                        m = mm(ps[:, b, g * 64:(g + 1) * 64], sil[:, g * 128:(g + 1) * 128], w2[rows, :], True, True, e, f, sm_t, signal=True)
                    put(tmps, sl, m)
                    vc_tok[0] = act(vcmp, ps[:, b, 0:128], ACT.Copy, m, vcf)
                    put(banks, b, vc_tok[0])
                    for z in range(24, 31):
                        put(tmps, z, all_done())
                    for z in (kt1, kt2):
                        put(tmps, z, all_done())

            win_free = [None]
            ctab_t = None
            a = [tt("pool", ctab[0:32, 0:64], ctab[0:32, 0:64], tmp[0:32, g_, 64:128], ALU.mult, sm_t, gain_t)]
            for h in range(2):
                o_ = 64 + 32 * (1 - h)
                a += [tt("pool", ctab[0:32, 64 + 32 * h:96 + 32 * h], ctab[0:32, 64 + 32 * h:96 + 32 * h],
                       tmp[0:32, g_, o_:o_ + 32], ALU.mult, sm_t, gain_t)]
            ctab_t = a
            tmps[:] = [(i, tk) if i != g_ else (i, [tk, a]) for i, tk in tmps]

            def compressed():
                while kc_tok[0] is None or gate_tok[0] is None or any(t is None for t in qT_tok):
                    yield "held"
                yield [kc_tok[0], qT_tok, gate_tok[0]]
                tr = [get(banks) for _ in range(2)]
                for t in range(4):
                    b, f = get(banks)
                    out4 = ps[:, b, 0:256].rearrange("p (g i n) -> p g i n", g=2, i=4)
                    for i in range(4):
                        m = mm(out4[:, :, i, :], qT[:, i, t * 128:(t + 1) * 128], kcT.rearrange("p (g n) -> p g n", g=2), True, True,
                               kc_tok[0], qT_tok, f, signal=i == 3)
                    z, zf = get(tmps)
                    st, sf = get(smalls)
                    p = tmp[:, z, 0:256].rearrange("p (h n) -> p h n", n=32)
                    bc = cmpmask[:, t * 32:t * 32 + 32].unsqueeze(1).to_broadcast([128, 8, 32])
                    mc = cmpmask[:, 128 + t * 32:128 + t * 32 + 32].unsqueeze(1).to_broadcast([128, 8, 32])
                    r = stt(p, ps[:, b, 0:256].rearrange("p (h n) -> p h n", n=32), 0.125, bc, ALU.mult, ALU.add, m, mk_t, zf)
                    put(banks, b, r)
                    mx, dn = small[:, st, 0:8], small[:, st, 8:16]
                    r = reduce(mx, p, ALU.max, r, sf)
                    r = tt("dve", p, p, mx.unsqueeze(2).to_broadcast([128, 8, 32]), ALU.subtract, r)
                    r = act(p, p, ACT.Exp, r)
                    d = reduce(dn, p, ALU.add, r)
                    pm = tt("pool", p, p, mc, ALU.mult, r, d, mk_t)
                    d = recip(dn, dn, d)
                    d = tt("dve", dn, dn, gate_t[:, t, 0, :], ALU.mult, d, gate_tok[0])
                    r = tt("dve", p, p, dn.unsqueeze(2).to_broadcast([128, 8, 32]), ALU.mult, d, pm)
                    put(smalls, st, r)
                    yield [r]
                    for g in range(2):
                        m = transpose(ps[:, tr[g][0], t * 128:(t + 1) * 128], tmp[:, z, g * 128:(g + 1) * 128], r, tr[g][1],
                                      signal=True)
                    put(tmps, z, m)
                for g in range(2):
                    pc_tok[g] = act(S(pc[g]), B(tr[g][0]), ACT.Copy, m, pcf[g])
                    put(banks, tr[g][0], pc_tok[g])

            def head_pair(i):
                while any(t is None for t in qT_tok + kT_tok) or vc_tok[0] is None or pairs[0] < i - 1:
                    yield "held"
                yield [qT_tok, kT_tok]
                st = []
                po = {}
                halves = slice(0, 64), slice(64, 128)
                for br in range(2):
                    s_, sf = get(smalls)
                    zs, et, m = yield from softmax_scores([qT[r, i, :] for r in halves], [kT[r, br, :] for r in halves], S(bias_),
                                                          [small[:, s_, 8 * g:8 * g + 8] for g in range(2)],
                                                          qT_tok, kT_tok, bias_t, sf)
                    es = []
                    for g in range(2):
                        den = small[:, s_, 8 * g + 4:8 * g + 8]
                        r = recip(den, den, et[g])
                        hd = 4 * g + i
                        gv = gate_t[:, :, 1 + br, hd]
                        r = tt("dve", den, den, gv, ALU.mult, r, gate_tok[0])
                        es.append(softmax_scale(zs[g], [den[:, t:t + 1] for t in range(4)], r))
                    put(smalls, s_, es)
                    for g in range(2):
                        yield es[g]
                        po[br, g] = transposed(zs[g], es[g])
                    if br == 0:
                        while pc_tok[1] is None:
                            yield "held"
                    yield [po[br, 0][1], po[br, 1][1], pc_tok, vc_tok[0]]
                    if br == 0:
                        o, of = get(banks)
                        for g in range(2):
                            m = mm(ps[64 * g:64 * g + 64, o, :], vcmp[32 * i:32 * i + 32, g * 64:(g + 1) * 64],
                                   tmp[32 * i:32 * i + 32, pc[g], :], True, False, pc_tok, vc_tok[0], of)
                    parts = []
                    for g in range(2):
                        col = 128 * br + 64 * g
                        parts.append((po[br, g][0], po[br, g][1], lambda kt, col=col: vsw[:, kt, col:col + 64], vs_tok))
                    m = values(o, None, parts, False, br == 1)
                to_mix(4 + i, o, m)
                pairs[0] += 1

            pairs = [0]

            def pooled(gi, b, m):
                w = 2 << gi
                (u, uf), (s_, sf) = get(tmps), get(tmps)
                a = act(S(u), B(b), ACT.Copy, m, uf)
                put(banks, b, a)
                cur, cur_t = u, a
                nxt = s_
                (s2, s2f) = get(tmps)
                sh = 1
                while sh < w:
                    r1 = tt("pool", tmp[:, nxt, sh:T], tmp[:, cur, sh:T], tmp[:, cur, 0:T - sh], ALU.add, cur_t, sf, s2f)
                    r2 = op("pool", lambda e, nxt=nxt, cur=cur, sh=sh: e.tensor_copy(tmp[:, nxt, 0:sh], tmp[:, cur, 0:sh]), cur_t, sf, s2f)
                    cur_t = [r1, r2]
                    cur, nxt = nxt, (s2 if nxt == s_ else s_)
                    sh *= 2
                r1 = tt("dve", tmp[:, cur, 0:16], tmp[:, cur, 0:16], nsm[:, 228 + 16 * gi:244 + 16 * gi], ALU.mult, cur_t, sm_t)
                r1 = tt("dve", tmp[:, cur, 0:16], tmp[:, cur, 0:16], tmp[:, u, 0:16], ALU.subtract, r1)
                r2 = stt(tmp[:, cur, 16:T], tmp[:, cur, 16:T], 1.0 / w, tmp[:, u, 16:T], ALU.mult, ALU.subtract, cur_t)
                yield [r1, r2, pw_t]
                b, f = get(banks)
                m = mm(B(b), poolw[:, gi, :], S(cur), True, True, r1, r2, pw_t, f, signal=True)
                put(tmps, u, m)
                put(tmps, s_, m)
                put(tmps, s2, m)
                hi = act(a0h[:, gi, :], B(b), ACT.Copy, m, a_free[0], sm_t, scale=pscale[:, gi:gi + 1])
                lo = stt(a0l[:, gi, :], B(b), pscale[:, gi:gi + 1], f32(a0h[:, gi, :]), ALU.mult, ALU.subtract, hi, sm_t)
                put(banks, b, lo)
                a_tok[0][gi] = [hi, lo]

            running = []

            def dense():
                yield from v_units(lambda: None, h_mov(), take_q)
                b, m = project()
                running.append(windows(0, b, m))
                yield
                b, m = project()
                running.append(windows(1, b, m))
                yield
                b, m = project_gates()
                running.append(gates(b, m))
                yield
                yield from v_units(lambda: None, h_mov(), take_kv)
                running.append(compressed())
                for i in range(4):
                    running.append(head_pair(i))
                for i in range(4):
                    b, m = project()
                    running.append(pooled(i, b, m))
                    yield
                lend_h()
                yield from out_proj(list(range(8)), lambda d: mod[:, l, 2, d:d + 1], "sum")

            schedule(dense(), running, 99)
            for z in (mk_, bias_, vc, pc[0], pc[1], gs):
                put(tmps, z, all_done())
            give_back()
            nsa_free[0] = all_done()

        nsa_free = [None]

        def project_gates():
            b, free = get(banks)
            wi = take()
            c = wi % NCV
            hi, lo = cv_tok[wi]
            for k in range(KT):
                mh, ml, mt = h_mov()[k]
                w_h, w_l = wh[:, c, k * 24:k * 24 + 128], wl[:, c, k * 24:k * 24 + 128]
                mm(B(b), w_h, mh, k == 0, False, mt, hi, free)
                mm(B(b), w_h, ml, False, False)
                m = mm(B(b), w_l, mh, False, k == KT - 1, lo, signal=k == KT - 1)
            release(wi, m)
            h_free[0] = m
            return b, m

        def relu2(l, last):
            def up(p):
                ah, al = ahl[p % 2]

                def take_unit(t, b, m):
                    i, f = get(tmps)
                    r = act(S(i), B(b), ACT.Relu, m, f)
                    put(banks, b, r)
                    r = tt("pool", S(i), S(i), S(i), ALU.mult, r)
                    hi = act(ah[:, t, :], S(i), ACT.Copy, r, a_free[p % 2])
                    lo = tt("dve", al[:, t, :], S(i), f32(ah[:, t, :]), ALU.subtract, hi)
                    put(tmps, i, lo)
                    a_tok[p % 2][t] = [hi, lo]

                t = 0
                if p == 0:
                    four = [(get(banks), take()) for _ in range(4)]
                    for k in range(KT):
                        ms = [unit_mm(b, wi, h_mov(), [k], k == 0, k == KT - 1, f) for (b, f), wi in four]
                    for (b, f), wi in four:
                        release(wi, ms[t])
                        take_unit(t, b, ms[t])
                        t += 1
                while t < 8:
                    b, m = project()
                    take_unit(t, b, m)
                    t += 1

            def down(p):
                ah, al = ahl[p % 2]
                mov = [(ah[:, k, :], al[:, k, :], a_tok[p % 2][k]) for k in range(KT)]
                for d in range(KT):
                    b, free = get(banks)
                    wi = take()
                    m = unit_mm(b, wi, mov, range(KT), True, True, free)
                    release(wi, m)
                    xt[d] = stt(x[:, d, :], B(b), mod[:, l, 5, d:d + 1], x[:, d, :], ALU.mult, ALU.add, m, xt[d], xr[d],
                                mod_tok[l][5])
                    put(banks, b, xt[d])
                    if p == 3:
                        if last:
                            outs.append(dma(out[d], x[:, d, :], f"out{d}", xt[d]))
                        else:
                            sum_tile(d)
                a_free[p % 2] = m

            up(0), up(1), down(0), up(2), down(1), up(3), down(2), down(3)

        def memset(ap, v):
            return op("dve", lambda e: e.memset(ap, v))
        memset(ones[:, :], 1.0 / 1024)
        memset(eps[:, 0:1], 1e-6)
        memset(eps[:, 1:2], 1e-5)
        memset(one[:, :], 1.0)
        made = list(range(len(ops)))
        gt = [dma(gains[:, :, :], ins["gains"], "gains")]
        for d in range(KT):
            xt[d] = dma(x[:, d, :], ins["x"][d], f"x{d}")
            if d == 0:
                load_to(2)
        load_to(NRAW)
        gt.append(dma(ident[:, :], ins["ident"], "ident"))
        gt.append(dma(headones[:, :], ins["headones"], "headones"))
        gt.append(dma(gn_g[:, :], ins["gn"], "gn"))
        gt.append(dma(c_act[:, :], ins["c"], "c"))
        gt.append(dma(b_mod[:, :, :, :], ins["b_mod"], "b_mod"))
        gt.append(dma(norm_g[:, :, :, :], ins["norm_g"], "norm_g"))
        const_tok = [made] + gt
        wait("act", made, gt[0])
        wait("dve", gt[0])
        for d in range(KT):
            norm_tile(d, 0)
        outs = []
        background[0] = modulation()
        swiglu(1)
        wait("act", const_tok)
        wait("dve", const_tok)
        wait("pe", const_tok)
        if stop >= 2:
            hyb(2)
        if stop >= 3:
            swiglu(3)
        if stop >= 4:
            swiglu(4)
        if stop >= 5:
            stick(5)
        if stop >= 6:
            swiglu("final")
            final = final_norm_finish()
            if stop == 6:
                final_norm_scale(final)
        for l in range(2):
            if stop >= 8 + l:
                if l == 1:
                    norm_finish(True)
                modulated(l, 0, None if l else gains[:, 6, :])
                if l == 0:
                    final_norm_scale(final)
                hybrid(l)
                norm_finish(True)
                modulated(l, 1)
                relu2(l, l == 1)
        if not outs:
            for d in range(KT):
                outs.append(dma(out[d], x[:, d, :], f"out{d}", xt[d]))
        users = [[] for _ in ops]
        for i, (_, _, deps, _, _, _) in enumerate(ops):
            for d in deps:
                users[d].append(i)
        due = list(end)
        for i in range(len(ops) - 1, -1, -1):
            if users[i]:
                due[i] = min(begin[u] if ops[u][0] in ("pe", "sp") else due[u] - ops[u][3] for u in users[i])

        left = [len(deps) for _, _, deps, _, _, _ in ops]
        at_ = [0.0] * len(ops)
        done = [0.0] * len(ops)
        can = {k: [] for k in clock}
        now = {k: 0.0 for k in clock}
        nxt = {k: [i for i, o in enumerate(ops) if o[0] == k] for k in ("pe", "sp")}
        for k in nxt:
            nxt[k].reverse()
        order_of = {k: [] for k in clock}
        loaded = [None]

        def free(i):
            if ops[i][0] is None:
                finish(i, at_[i])
            elif ops[i][0] not in nxt:
                can[ops[i][0]].append(i)

        def finish(i, t):
            done[i] = t
            for u in users[i]:
                at_[u] = max(at_[u], t + 0.05)
                left[u] -= 1
                if left[u] == 0:
                    free(u)

        for i in [i for i in range(len(ops)) if left[i] == 0]:
            free(i)

        def best(k):
            if k in nxt:
                if not nxt[k] or left[nxt[k][-1]]:
                    return None
                i = nxt[k][-1]
                return (max(now[k], at_[i]), 0.0, i)
            pick = None
            for i in can[k]:
                start = max(now[k], at_[i])
                if k == "act" and ops[i][5] not in (None, loaded[0]):
                    start = max(now[k] + 1.3, at_[i])
                key = (start, due[i], i)
                if pick is None or key < pick:
                    pick = key
            return pick

        while True:
            picks = [(best(k), k) for k in clock]
            picks = [(p, k) for p, k in picks if p is not None]
            if not picks:
                break
            (start, _, i), k = min(picks)
            lane, call, deps, cost, sem, tab = ops[i]
            if k in nxt:
                nxt[k].pop()
            else:
                can[k].remove(i)
            if k == "act" and tab is not None and tab != loaded[0]:
                loaded[0] = tab
                order_of[k].append(("table", tab))
            order_of[k].append(("op", i))
            now[k] = start + (0.7 if sem else cost)
            finish(i, start + cost + 0.1)
        assert not any(left)

        sems, count, value = {}, {}, {}

        def count_up(i, name, n):
            if name not in sems:
                sems[name] = ctx.enter_context(nc.semaphore(name))
                count[name] = 0
            count[name] += n
            value[i] = (name, count[name])

        def wanted(i):
            return any(ops[u][0] is not None or wanted(u) for u in users[i])

        for k in order_of:
            for kind, i in order_of[k]:
                if kind == "op" and (ops[i][4] or wanted(i)):
                    count_up(i, ops[i][4] or k, 16 if ops[i][4] else 1)

        def through(i, into):
            if ops[i][0] is None:
                for d in ops[i][2]:
                    through(d, into)
            else:
                name, v = value[i]
                into[name] = max(into.get(name, 0), v)
            return into

        block = ctx.enter_context(nc.Block())

        def play(lane, eng):
            seen = {}
            for kind, i in order_of[lane]:
                if kind == "table":
                    eng.preload_act_table_set(i)
                    continue
                need = {}
                for d in ops[i][2]:
                    through(d, need)
                for name, v in sorted(need.items()):
                    if seen.get(name, 0) < v:
                        seen[name] = v
                        eng.wait_ge(sems[name], v)
                made_ = ops[i][1](eng)
                if i in value:
                    made_.then_inc(sems[value[i][0]], 16 if ops[i][4] else 1)
            if lane == "sp":
                for i in outs:
                    eng.wait_ge(sems[value[i][0]], value[i][1])

        @block.sync
        def _(e):
            play("sp", e)

        @block.tensor
        def _(e):
            play("pe", e)

        @block.vector
        def _(e):
            play("dve", e)

        @block.scalar
        def _(e):
            play("act", e)

        @block.gpsimd
        def _(e):
            play("pool", e)


HYB_ORDER = [("d", 0), ("d", 1), ("d", 2), ("d", 3), ("r", 0), ("r", 1), ("g", 0), ("r", 2), ("g", 1), ("r", 3),
             ("g", 2), ("g", 3)]


def pack(w):
    k, n = w.shape
    return np.ascontiguousarray(w.reshape(k // 128, 128, n // 128, 128).transpose(2, 1, 0, 3).reshape(n // 128, 128, k))


def pack_tokens(w):
    return np.ascontiguousarray(w.reshape(4, 2, 128, 512).transpose(0, 2, 1, 3).reshape(4, 128, 1024))


def rope_perm():
    return np.concatenate([np.arange(0, 16), np.arange(32, 48), np.arange(16, 32), np.arange(48, 64)])


def tables():
    f = np.float32
    a = {}
    t = np.arange(512, dtype=f)
    inv = f(1) / (f(10000.0) ** (np.arange(32, dtype=f) / f(32)))
    ang = (t[None, :] * inv[:, None]).astype(f)
    d = rope_perm()
    cos, sin = np.cos(ang).astype(f), np.sin(ang).astype(f)
    rc = cos[d % 32]
    rs = sin[d % 32] * np.where(d < 32, -1, 1)[:, None].astype(f)
    inv = f(1) / (f(500000.0) ** (np.arange(8, dtype=f) / f(8)))
    ang = (t[None, :] * inv[:, None]).astype(f)
    dc, ds = np.ones((64, 512), f), np.zeros((64, 512), f)
    dc[0:16] = np.cos(ang).astype(f)[np.arange(16) % 8]
    ds[0:16] = np.sin(ang).astype(f)[np.arange(16) % 8] * np.where(np.arange(16) < 8, -1, 1)[:, None].astype(f)
    a["rope"] = np.ascontiguousarray(np.stack([np.tile(z, (2, 1)) for z in (rc, rs, dc, ds)], 1))
    q, k = np.arange(128)[:, None], np.arange(512)[None, :]
    dist = q + 384 - k
    c = ((dist >= 0) & (dist <= 128)).astype(int) + ((dist >= 0) & (dist % 4 == 0)) + ((dist >= 0) & (dist % 16 == 0))
    a["dilbias"] = np.where(c > 0, 8 * np.log(np.maximum(c, 1)), -1e30).astype(f)
    g = 1.0 - 2.0 ** (-5.0 - np.arange(8))
    j, i = np.arange(128)[:, None], np.arange(512)[None, :]
    a["decay"] = np.stack([np.where(i >= j, 0.125 * gg ** np.maximum(i - j, 0), 0) for gg in g]).astype(f)
    a["ident"] = np.eye(128, dtype=f)
    inv = f(10000.0) ** (-np.arange(32, dtype=f) * f(2.0) / f(64))
    ang = (np.arange(512, dtype=f)[:, None] * inv[None, :]).astype(f)
    c, s = np.cos(ang).astype(f), np.sin(ang).astype(f)
    cos2, sin2 = np.concatenate([c, c], 1), np.concatenate([-s, s], 1)
    a["rope2"] = np.ascontiguousarray(np.stack([cos2, sin2], 0).reshape(2, 4, 128, 64).transpose(2, 0, 1, 3).reshape(128, 512))
    q, n = np.arange(512)[:, None], np.arange(32)[None, :]
    ok = (16 * n + 31 <= q) & (n < 31)
    m = np.stack([np.where(ok, 0, -1e30), np.where(ok, 1, 0)], 0).astype(f)
    m = np.where((n >= 31) & (np.arange(2) == 0)[:, None, None], f(-2e30), m)
    a["cmp_mask"] = np.concatenate([m.reshape(2, 4, 128, 32).transpose(2, 0, 1, 3).reshape(128, 256), np.zeros((128, 256), f)], 1)
    qq, kk = np.arange(128)[:, None], np.arange(512)[None, :]
    a["causal"] = np.where(kk <= qq + 384, 0, -1e30).astype(f)
    end = np.minimum(16 * np.arange(32) + 31, 511)
    ctab = np.zeros((128, 128), f)
    ctab[0:32] = np.concatenate([cos2[end], sin2[end]], 1)
    inv_count = np.concatenate([1.0 / np.minimum(np.arange(16) + 1, w) for w in (2, 4, 8, 16)]).astype(f)
    a["_ctab"], a["_inv_count"] = ctab, inv_count
    i, j = np.arange(128)[:, None], np.arange(128)[None, :]
    a["sbmask"] = np.ascontiguousarray(np.concatenate([np.eye(128), np.where(i < j, 0, -1e30)], 1)).astype(f)
    a["headones"] = (np.kron(np.eye(2), np.ones((64, 64))) / 64).astype(f)
    return a


def lay(inp):
    a = {}
    a["x"] = np.ascontiguousarray(inp["x"][0].T).reshape(8, 128, 512)

    def gate_up(w):
        g, u = pack(w[:, :2816]), pack(w[:, 2816:])
        return np.ascontiguousarray(np.stack([g, u], 1).reshape(44, 128, 1024))
    for n, key in (("f1", "ffn1"), ("f2", "ffn2")):
        a[n + "i"] = np.stack([gate_up(w) for w in inp[key + "_w_in"]])
        a[n + "o"] = np.stack([pack(w) for w in inp[key + "_w_out"]])
    gains = np.stack([inp["ffn1_norm"][0], inp["mix_norm"][0], inp["ffn2_norm"][0],
                      inp["ffn1_norm"][1], inp["mix_norm"][1], inp["ffn2_norm"][1], inp["final_norm"]])
    a["gains"] = np.ascontiguousarray(gains.reshape(7, 8, 128).transpose(2, 0, 1))
    w = inp["hyb_w_in"][0]
    perm = np.concatenate([h * 64 + rope_perm() for h in range(8)])
    rq, rk, rv, rg, dq, dk, dv = [w[:, i * 512:(i + 1) * 512] for i in range(7)]
    rq, rk, rg, dq, dk = pack(rq[:, perm]), pack(rk[:, perm]), pack(rg), pack(dq), pack(dk)
    units = list(pack_tokens(dv)) + list(pack_tokens(rv))
    for kind, p in HYB_ORDER:
        units += {"d": [dq[p], dk[p]], "r": [rq[p], rk[p]], "g": [rg[p]]}[kind]
    a["hyb"] = np.stack(units)
    a["hybo"] = pack(inp["hyb_w_out"][0])
    w = inp["sb_w_in"][0]
    q, k = pack(w[:, :1024]), pack(w[:, 1024:2048])
    units = list(pack_tokens(w[:, 2048:2560])) + list(pack_tokens(w[:, 2560:]))
    for p in range(8):
        units += [q[p], k[p]]
    a["sb"] = np.stack(units)
    a["sbo"] = pack(inp["sb_w_out"][0])
    a["gn"] = np.ascontiguousarray(inp["ret_gn"][0].reshape(4, 128).T)
    a.update(tables())
    hp = [0, 4, 1, 5, 2, 6, 3, 7]
    nsa, gates, small = [], [], []
    for l in range(2):
        w = inp["w_in_2"][l]
        u, q, kv, g = w[:, :512], w[:, 512:1024].reshape(1024, 8, 64), w[:, 1024:1792], w[:, 1792:]
        q = q[:, hp].reshape(1024, 512)
        kc, ks, kw, vc, vs, vw = [kv[:, i * 128:(i + 1) * 128] for i in range(6)]
        nsa.append(np.concatenate([pack_tokens(q), pack(kc), pack(vc), pack_tokens(np.concatenate([ks, kw, vs, vw], 1)), pack(u)]))
        g = g.reshape(8, 128, 8, 3).transpose(1, 0, 3, 2).reshape(128, 192)
        gates.append(np.concatenate([g, np.zeros((128, 128), np.float32)], 1))
        pe = inp["cmp_pe_2"][l].reshape(2, 16, 128).transpose(2, 0, 1).reshape(128, 32)
        w2 = inp["cmp_w2_2"][l].reshape(128, 64)
        psc = inp["pool_scale_2"][l].reshape(4, 128).T
        small.append(np.concatenate([pe, w2, psc, a["_ctab"], np.tile(a["_inv_count"], (128, 1))], 1))
    a["nsa"], a["gates"], a["nsa_small"] = np.stack(nsa), np.stack(gates), np.stack(small)
    del a["_ctab"], a["_inv_count"]
    gain = np.concatenate([inp["q_norm_2"][:, None], inp["k_norm_2"]], 1).reshape(2, 1, 256)
    a["qk_gain"] = np.ascontiguousarray(np.broadcast_to(gain, (2, 128, 256)))
    a["cmp_w1"] = np.ascontiguousarray(inp["cmp_w1_2"].reshape(2, 2, 16, 128, 64).transpose(0, 3, 1, 2, 4))
    a["pool_w"] = np.ascontiguousarray(inp["pool_w_2"].transpose(0, 2, 1, 3))
    rows = np.concatenate([np.arange(512)] + [512 + h * 64 + np.arange(64) for h in hp])
    a["mixo"] = np.stack([pack(w[rows]) for w in inp["w_out_2"]])
    a["ff1"] = np.stack([pack(w) for w in inp["w_ff1_2"]])
    a["ff2"] = np.stack([pack(w) for w in inp["w_ff2_2"]])
    a["w_mod"] = inp["w_mod_2"]
    a["b_mod"] = np.ascontiguousarray(inp["b_mod_2"].reshape(2, 6, 8, 128).transpose(3, 0, 1, 2))
    a["norm_g"] = np.ascontiguousarray(np.stack([inp["norm1_2"], inp["norm2_2"]], 1).reshape(2, 2, 8, 128).transpose(3, 0, 1, 2))
    a["c"] = np.ascontiguousarray(inp["c_2"].reshape(8, 128).T)
    return a


def kernel(**inputs):
    import concourse.bacc as bacc
    from concourse.bass_utils import run_bass_kernel_spmd

    arrays = lay({k: np.asarray(v) for k, v in inputs.items()})
    nc = bacc.Bacc("TRN2", target_bir_lowering=False, num_devices=1)
    ins, given = {}, {}
    for name, a in arrays.items():
        a = np.ascontiguousarray(a)
        given[f"in_{name}_dram"] = a
        ins[name] = nc.dram_tensor(f"in_{name}_dram", a.shape, mybir.dt.from_np(a.dtype), kind="ExternalInput").ap()
    out = nc.dram_tensor("out_0_dram", (8, 128, 512), mybir.dt.float32, kind="ExternalOutput").ap()
    two_block_kernel(nc, ins, out)
    r = run_bass_kernel_spmd(nc, [given], core_ids=[0])
    y = np.asarray(r.results[0]["out_0_dram"]).reshape(1024, 512)
    return np.ascontiguousarray(y.T).reshape(1, 512, 1024)
```
